# Optimizing a Trainium2 kernel written in Bass

```python
import jax, jax.numpy as jnp
from jax import lax
import numpy as np

D_MODEL = 1024
BATCH = 1
SEQ = 512
DEPTH = 2
DEC_BATCH = 8
DEC_SEQ = 4
PAST_LEN = 4096
PAGE_SIZE = 128

MIX_WIDTH = D_MODEL
HEAD_DIM = 64
A_HEADS = 4
A_WIDTH = A_HEADS * HEAD_DIM
A_CHUNK = 128
B_GROUPS = 4
B_WIDTH = MIX_WIDTH // 4
CONV_W = 3
C_HEADS = 8
C_WIDTH = C_HEADS * HEAD_DIM
RET_CHUNK = 128
ROPE_BASE = 10000.0
D_FF = -(-8 * D_MODEL // (3 * 256)) * 256
IN_COLS = 2 * A_WIDTH + 3 * B_WIDTH + 4 * C_WIDTH
EPS = 1e-6

kernel_name = 'hybrid_gmlp_shortconv_retention_step'

def rmsnorm(x, g):
    xf = x.astype(jnp.float32)
    y = xf * lax.rsqrt(jnp.mean(xf * xf, -1, keepdims=True) + EPS)
    return (y * g.astype(jnp.float32)).astype(x.dtype)

def layernorm(x, g, b):
    xf = x.astype(jnp.float32)
    mu = jnp.mean(xf, -1, keepdims=True)
    xc = xf - mu
    y = xc * lax.rsqrt(jnp.mean(xc * xc, -1, keepdims=True) + EPS)
    return (y * g.astype(jnp.float32) + b.astype(jnp.float32)).astype(x.dtype)

def split_cols(p):
    sizes = [A_WIDTH] * 2 + [B_WIDTH] * 3 + [C_WIDTH] * 4
    offs, acc = [], 0
    for s in sizes[:-1]:
        acc += s
        offs.append(acc)
    return jnp.split(p, offs, axis=-1)

def chunk_mlp(u, v, w_s, b_s, ln_g, ln_b):
    bt, L, _ = u.shape
    n = min(A_CHUNK, L)
    vn = layernorm(v, ln_g, ln_b)
    vh = vn.reshape(bt, L // n, n, A_HEADS, HEAD_DIM)
    w = w_s[:, :n, :n] * jnp.tril(jnp.ones((n, n), w_s.dtype))
    mixed = jnp.einsum('hij,bcjhd->bcihd', w, vh) + jnp.transpose(b_s[:, :n])[None, None, :, :, None]
    return u * mixed.reshape(bt, L, A_WIDTH), vn.reshape(bt, L, A_HEADS, HEAD_DIM)

def short_conv(bg, cg, xb, conv_w, buf):
    L = xb.shape[1]
    z = cg * xb
    zp = jnp.concatenate([buf.astype(z.dtype), z], axis=1)
    y = zp[:, 0:L] * conv_w[0]
    for tap in range(1, CONV_W):
        y = y + zp[:, tap:tap + L] * conv_w[tap]
    return bg * y, zp[:, -(CONV_W - 1):]

def rope(x, pos):
    half = x.shape[-1] // 2
    inv = ROPE_BASE ** (-jnp.arange(half, dtype=jnp.float32) / half)
    ang = pos[:, None] * inv[None, :]
    cos = jnp.cos(ang)[None, :, None, :]
    sin = jnp.sin(ang)[None, :, None, :]
    x1, x2 = x[..., :half], x[..., half:]
    return jnp.concatenate([x1 * cos - x2 * sin, x2 * cos + x1 * sin], axis=-1)

def retention_scan(q, k, v, s0):
    bt, L, H, d = q.shape
    c = min(RET_CHUNK, L)
    n = L // c
    log_g = jnp.log(1.0 - 2.0 ** (-5.0 - jnp.arange(H, dtype=jnp.float32)))
    i = jnp.arange(c, dtype=jnp.float32)
    diff = i[:, None] - i[None, :]
    dmask = jnp.where(diff >= 0, jnp.exp(log_g[:, None, None] * jnp.maximum(diff, 0.0)), 0.0)
    q_dec = jnp.exp(log_g[None, :] * (i[:, None] + 1.0))
    k_dec = jnp.exp(log_g[None, :] * (c - 1.0 - i)[:, None])
    chunk_dec = jnp.exp(log_g * c)

    def to_chunks(t):
        return t.reshape(bt, n, c, H, d).transpose(1, 0, 2, 3, 4)

    def step(S, qkv):
        qc, kc, vc = qkv
        sc = jnp.einsum('bihd,bjhd->bhij', qc, kc) * dmask[None]
        o = jnp.einsum('bhij,bjhe->bihe', sc, vc) + jnp.einsum('bihd,bhde->bihe', qc * q_dec[None, :, :, None], S)
        S = chunk_dec[None, :, None, None] * S + jnp.einsum('bjhd,bjhe->bhde', kc * k_dec[None, :, :, None], vc)
        return S, o

    S, o = lax.scan(step, s0, (to_chunks(q), to_chunks(k), to_chunks(v)))
    return o.transpose(1, 0, 2, 3, 4).reshape(bt, L, H, d), S

def retention(q, k, v, g, s0, pos0):
    bt, L, _ = q.shape
    f32 = jnp.float32
    pos = jnp.arange(L, dtype=f32) + pos0
    qh = rope(q.astype(f32).reshape(bt, L, C_HEADS, HEAD_DIM), pos) * (HEAD_DIM ** -0.5)
    kh = rope(k.astype(f32).reshape(bt, L, C_HEADS, HEAD_DIM), pos)
    vh = v.astype(f32).reshape(bt, L, C_HEADS, HEAD_DIM)
    o, S = retention_scan(qh, kh, vh, s0.astype(f32))
    o = o * lax.rsqrt(jnp.mean(o * o, -1, keepdims=True) + EPS)
    out = o.reshape(bt, L, C_WIDTH) * jax.nn.silu(g.astype(f32))
    return out.astype(q.dtype), S

def layer(x, conv_buf, ret_s, pos0, w_in, w_out, w_s, b_s, ln_g, ln_b, conv_w,
          g_pre_mix, g_post_mix, g_pre_ffn, g_post_ffn, w_gate, w_up, w_down):
    h = rmsnorm(x, g_pre_mix)
    p = jnp.einsum('bld,dc->blc', h, w_in)
    a_u, a_v, b_b, b_c, b_x, c_q, c_k, c_v, c_g = split_cols(p)
    a_out, a_vrows = chunk_mlp(a_u, a_v, w_s, b_s, ln_g, ln_b)
    b_out, new_buf = short_conv(b_b, b_c, b_x, conv_w, conv_buf)
    c_out, new_s = retention(c_q, c_k, c_v, c_g, ret_s, pos0)
    m = jnp.einsum('blc,cd->bld', jnp.concatenate([a_out, b_out, c_out], axis=-1), w_out)
    x = x + rmsnorm(m, g_post_mix)
    h = rmsnorm(x, g_pre_ffn)
    f = jax.nn.silu(h @ w_gate) * (h @ w_up)
    x = x + rmsnorm(f @ w_down, g_post_ffn)
    return x, a_vrows, new_buf, new_s.astype(x.dtype)

def setup_inputs(seed: int = 0) -> dict:
    key = jax.random.key(seed)
    ks = jax.random.split(key, 24)
    nrm = jax.random.normal
    f32 = jnp.float32
    return {
        'x_prompt': nrm(ks[0], (BATCH, SEQ, D_MODEL), f32),
        'x_sample': nrm(ks[1], (DEC_BATCH, DEC_SEQ, D_MODEL), f32),
        'state_ret': nrm(ks[2], (DEPTH, DEC_BATCH, C_HEADS, HEAD_DIM, HEAD_DIM), f32),
        'state_conv': nrm(ks[3], (DEPTH, DEC_BATCH, CONV_W - 1, B_WIDTH), f32),
        'w_in': nrm(ks[4], (DEPTH, D_MODEL, IN_COLS), f32) * D_MODEL ** -0.5,
        'w_out': nrm(ks[5], (DEPTH, MIX_WIDTH, D_MODEL), f32) * MIX_WIDTH ** -0.5,
        'w_s': nrm(ks[6], (DEPTH, A_HEADS, A_CHUNK, A_CHUNK), f32) * A_CHUNK ** -0.5,
        'b_s': 1.0 + 0.1 * nrm(ks[7], (DEPTH, A_HEADS, A_CHUNK), f32),
        'ln_g': 1.0 + 0.05 * nrm(ks[8], (DEPTH, A_WIDTH), f32),
        'ln_b': 0.02 * nrm(ks[9], (DEPTH, A_WIDTH), f32),
        'conv_w': nrm(ks[10], (DEPTH, CONV_W, B_WIDTH), f32) * CONV_W ** -0.5,
        'g_pre_mix': 1.0 + 0.05 * nrm(ks[11], (DEPTH, D_MODEL), f32),
        'g_post_mix': 1.0 + 0.05 * nrm(ks[12], (DEPTH, D_MODEL), f32),
        'g_pre_ffn': 1.0 + 0.05 * nrm(ks[13], (DEPTH, D_MODEL), f32),
        'g_post_ffn': 1.0 + 0.05 * nrm(ks[14], (DEPTH, D_MODEL), f32),
        'w_gate': nrm(ks[15], (DEPTH, D_MODEL, D_FF), f32) * D_MODEL ** -0.5,
        'w_up': nrm(ks[16], (DEPTH, D_MODEL, D_FF), f32) * D_MODEL ** -0.5,
        'w_down': nrm(ks[17], (DEPTH, D_FF, D_MODEL), f32) * D_FF ** -0.5,
    }

def reference(x_prompt, x_sample, state_ret, state_conv, w_in, w_out, w_s, b_s, ln_g, ln_b, conv_w,
              g_pre_mix, g_post_mix, g_pre_ffn, g_post_ffn, w_gate, w_up, w_down):
    yp, ys = x_prompt, x_sample
    rp, rs, cp, cs, vs = [], [], [], [], []
    for l in range(DEPTH):
        params = (w_in[l], w_out[l], w_s[l], b_s[l], ln_g[l], ln_b[l], conv_w[l],
                  g_pre_mix[l], g_post_mix[l], g_pre_ffn[l], g_post_ffn[l],
                  w_gate[l], w_up[l], w_down[l])
        buf0 = jnp.zeros((yp.shape[0], CONV_W - 1, B_WIDTH), yp.dtype)
        s0 = jnp.zeros((yp.shape[0], C_HEADS, HEAD_DIM, HEAD_DIM), jnp.float32)
        yp, _, buf_p, s_p = layer(yp, buf0, s0, 0, *params)
        ys, v_s, buf_s, s_s = layer(ys, state_conv[l], state_ret[l], PAST_LEN, *params)
        rp.append(s_p)
        rs.append(s_s)
        cp.append(buf_p)
        cs.append(buf_s)
        vs.append(v_s)
    return (yp, ys, jnp.stack(rp), jnp.stack(rs), jnp.stack(cp), jnp.stack(cs), jnp.stack(vs))


_drawn_inputs = setup_inputs


def setup_inputs(seed=0):
    import zlib

    import numpy as np

    out = dict(_drawn_inputs(seed))
    spreads = {}
    factors = {'ln_b': 2.877}
    for name, (base, spread) in spreads.items():
        noise = np.random.default_rng([zlib.crc32(name.encode()), seed]).standard_normal(out[name].shape)
        drawn = base * np.exp(spread * noise) if base else spread * noise
        out[name] = __import__('jax').numpy.asarray(drawn.astype(out[name].dtype))
    for name, factor in factors.items():
        out[name] = (out[name] * factor).astype(out[name].dtype)
    return out
```

```python
from contextlib import ExitStack

import numpy as np

import concourse.bass as bass
from concourse import mybir

F32 = mybir.dt.float32
F32R = mybir.dt.float32r
ACT = mybir.ActivationFunctionType
ALU = mybir.AluOpType

P = 128
DEPTH, D, FF = 2, 1024, 2816
SEQ, DB, DS = 512, 8, 4
NS = DB * DS
T = SEQ + NS
H2 = T // 2
CH = 128
NC = SEQ // CH
HEADS, HD, AHEADS = 8, 64, 4
HP = HEADS // 2
AW = BW = 256
INC = 3328
KT = D // P
FT = FF // P
EPS = 1e-6

K01, K23, V01, V23, Q01, Q23, AV, AU, BB, BC, BX, G01, G23 = range(13)
WIN_COLUMNS = [7, 8, 9, 10, 5, 6, 1, 0, 2, 3, 4, 11, 12]
N_WIN = 2 * len(WIN_COLUMNS)
N_WOUT = 8
N_FFN = 4 * (FF // 256)
DOWN = [(pair, sum(ks[:i]), nk)
        for pair, ks in enumerate(3 * [[4, 4, 4, 4, 4, 2]] + [[2, 2, 2, 2, 4, 4, 4, 2]])
        for i, nk in enumerate(ks)]
DOWN_TAIL = 3
N_DOWN = len(DOWN)
OUT0, FFN0, DOWN0 = N_WIN, N_WIN + N_WOUT, N_WIN + N_WOUT + N_FFN
UNITS = DOWN0 + N_DOWN
RING = 4
USES = [sum(1 for u in range(UNITS) if u % RING == s) for s in range(RING)]
LEAD = 2

TASKS_AFTER = {
    3: ["setup_weights"], 4: ["setup_rows"], 5: ["turn_k0"], 6: ["turn_k1"], 7: ["turn_k2", "turn_k3"],
    8: ["turn_v0", "turn_v1"], 9: ["turn_v2"], 10: ["turn_v3"], 13: ["scores0"], 14: ["turn_av"],
    15: ["turn_av_s"], 16: ["chunk0"], 17: ["mix_tokens", "norm_o0"], 18: ["chunk1"],
    19: ["mix_tokens_s", "norm_o1"], 20: ["chunk2"], 21: ["norm_o2"], 22: ["chunk3"],
    23: ["attend_s", "norm_o3"], 24: ["norm_o4", "state_s0"], 25: ["state_s1"],
}
TASK = {name: n + 1 for n, name in enumerate(t for ts in TASKS_AFTER.values() for t in ts)}
OUT_ORDER = [(0, 0), (1, 0), (0, 1), (1, 1), (2, 0), (2, 1), (3, 0), (3, 1)]
OUT_LAST = {2: 0, 3: 1, 5: 2, 7: 3}

G_PRE_MIX, G_POST_MIX, G_PRE_FFN, G_POST_FFN, CONV = 0, 8, 16, 24, 32
NPRM = 38

C_ID, C_BLK, C_CDEC, C_CDECS, C_KDEC, C_KDECS, C_BMASK, C_REP, C_SEL = 0, 128, 256, 260, 264, 272, 280, 288, 320
N_CONST = 576
T_DM, T_DMS, T_COS, T_SIN, T_QD, T_TRIL, T_TRILS = 0, 1024, 1280, 1824, 2368, 3008, 3136
N_TAB = 3168


def tables():
    f = np.float32
    log_g = np.log(1.0 - 2.0 ** (-5.0 - np.arange(HEADS)))
    scale = HD ** -0.5
    c = np.zeros((P, N_CONST), f)
    c[:, C_ID:C_ID + P] = np.eye(P)
    c[:, C_BLK:C_BLK + P] = np.kron(np.eye(2), np.full((HD, HD), 1.0 / HD))
    part_head = np.arange(P) // HD
    for hp in range(HP):
        c[:, C_CDEC + hp] = np.exp(log_g[2 * hp + part_head] * CH)
        c[:, C_CDECS + hp] = np.exp(log_g[2 * hp + part_head] * DS)
    j = np.arange(P)
    js = np.arange(NS)
    c[:, C_KDEC:C_KDEC + HEADS] = np.exp(log_g[None] * (CH - 1 - j)[:, None])
    c[:NS, C_KDECS:C_KDECS + HEADS] = np.exp(log_g[None] * (DS - 1 - js % DS)[:, None])
    c[:NS, C_BMASK:C_BMASK + DB] = js[:, None] // DS == np.arange(DB)[None]
    c[:DS, C_REP:C_REP + NS] = np.arange(DS)[:, None] == js[None] % DS
    for hp in range(2):
        for h in range(AHEADS):
            c[h, C_SEL + P * hp:C_SEL + P * (hp + 1)] = part_head + 2 * hp == h
    t = np.zeros((P, N_TAB), f)
    diff = j[None] - j[:, None]
    dm = np.where(diff[None] >= 0, np.exp(log_g[:, None, None] * np.maximum(diff, 0)[None]), 0) * scale
    order = sorted(range(HEADS), key=by_parity)
    t[:, T_DM:T_DM + 1024] = dm[order].transpose(1, 0, 2).reshape(P, -1)
    ds_ = js[None] - js[:, None]
    same = (js[None] // DS == js[:, None] // DS) & (ds_ >= 0)
    dms = np.where(same[None], np.exp(log_g[:, None, None] * np.maximum(ds_, 0)[None]), 0) * scale
    t[:NS, T_DMS:T_DMS + 256] = dms[order].transpose(1, 0, 2).reshape(NS, -1)
    half = HD // 2
    inv = (10000.0 ** (-np.arange(half) / half)).astype(f)
    pos = np.concatenate([np.arange(SEQ), np.tile(4096 + np.arange(DS), DB)]).astype(f)
    ang = (pos[None] * inv[j % half][:, None]).astype(f)
    sign = np.where((j // half) % 2 == 0, -1.0, 1.0)[:, None]
    t[:, T_COS:T_COS + T] = np.cos(ang)
    t[:, T_SIN:T_SIN + T] = np.sin(ang) * sign
    qi = np.concatenate([j, js % DS]) + 1.0
    for hp in range(HP):
        t[:, T_QD + 160 * hp:T_QD + 160 * (hp + 1)] = np.exp(log_g[2 * hp + part_head][:, None] * qi[None]) * scale
    t[:, T_TRIL:T_TRIL + P] = diff >= 0
    t[:NS, T_TRILS:T_TRILS + NS] = same
    return c, t


def by_parity(h):
    return 4 * (h % 2) + h // 2


class Signal:

    def __init__(self, sem, per_layer):
        self.sem, self.per, self.n = sem, per_layer, 0

    def at(self, layer, n):
        return layer * self.per + n


VEC_OWN = 37


class Own(Signal):

    def mark(self, ins):
        ins.then_inc(self.sem, 1)
        self.n += 1
        return self.n


def build(nc, x_prompt, x_sample, state_ret, state_conv, w_in, w_out, w_s, b_s, ln_g, ln_b, conv_w,
          g_pre_mix, g_post_mix, g_pre_ffn, g_post_ffn, w_gate, w_up, w_down, const, table,
          y_prompt, y_sample, ret_prompt, ret_sample, conv_prompt, conv_sample, chunkv_sample):
    ctx = ExitStack()
    with ctx:
        at = [(nc.sbuf_base + 31) // 32 * 32]

        def sb(name, shape, dt=F32, where=None):
            size = 4 * int(np.prod(shape[1:]))
            if where is None:
                where = at[0]
                at[0] += (size + 31) // 32 * 32
            buf = nc.alloc_sbuf_tensor_at(name, shape, dt, offset=where)
            place[name] = where
            return buf

        place = {}
        cst = sb("cst", [P, N_CONST])
        x = sb("x", [P, KT, T])
        prm_all = sb("prm_all", [P, DEPTH, NPRM])
        prm = sb("prm", [P, NPRM])
        prow = sb("prow", [2 * NPRM, P])
        eps = sb("eps", [P, 1])
        ones = sb("ones", [P, P])
        r_pre = sb("r_pre", [P, 1, T])
        r_post = sb("r_post", [P, 1, T])
        acc = sb("acc", [P, 2, T])
        E = [sb(f"evac{i}", [P, 2, T]) for i in range(2)]
        h_hi = sb("h_hi", [P, KT, T], F32R)
        h_lo = sb("h_lo", [P, KT, T], F32R)
        y = sb("y", [P, KT, T], F32, place["h_hi"])
        w_raw = [sb(f"w_raw{s}", [P, 4, 256]) for s in range(RING)]
        w_hi = [sb(f"w_hi{s}", [P, 4, 256], F32R) for s in range(RING)]
        w_lo = [sb(f"w_lo{s}", [P, 4, 256], F32R, place[f"w_raw{s}"]) for s in range(RING)]
        mix0 = at[0]
        f_hi = sb("f_hi", [P, FT, T], F32R)
        f_lo = sb("f_lo", [P, FT, T], F32R)
        ffn_end = at[0]
        at[0] = mix0
        tab = sb("tab", [P, N_TAB])
        v_tok = sb("v_tok", [P, NC + 1, 512])
        k_tok = sb("k_tok", [P, NC + 1, 512])
        qo = sb("qo", [P, HP, T])
        c_lo = sb("c_lo", [P, HP, T], F32R, place["qo"])
        kT = sb("kT", [P, HP, T])
        qd = sb("qd", [P, HP, CH], F32, place["r_post"])
        rn = sb("rn", [P, 2, HP, CH], F32, place["acc"])
        qds = sb("qds", [P, HP, NS])
        probs = sb("probs", [P, 2, HEADS, CH])
        ws_in = sb("ws_in", [P, AHEADS, CH], F32, place["probs"])
        vexp = sb("vexp", [NS, 4, DB, HD], F32, place["probs"])
        sg = sb("sg", [P, HP, T])
        c_hi = sb("c_hi", [P, HP, T], F32R, place["sg"])
        z_p = sb("z_p", [P, 2, SEQ + 2], F32, place["sg"])
        z_s = sb("z_s", [P, 2, DB, DS + 2], F32, place["sg"] + 4 * 2 * (SEQ + 2) + 16)
        a_u = sb("a_u", [P, 2, T])
        a_lo = sb("a_lo", [P, 2, T], F32R, place["a_u"])
        b_b = sb("b_b", [P, 2, T])
        b_lo = sb("b_lo", [P, 2, T], F32R, place["b_b"])
        ab_hi = sb("ab_hi", [P, 4, T], F32R)
        z_last = sb("z_last", [P, 2, 2 + 2 * DB])
        vn = sb("vn", [P, NC + 1, AW])
        ln_row = sb("ln_row", [1, 2, AW], F32, place["vn"])
        bs_row = sb("bs_row", [AHEADS, P], F32, place["vn"] + 2048)
        sc_in = sb("sc_in", [2 * DB, BW], F32, place["vn"] + 2560)
        st_p = sb("st_p", [P, HP, HD])
        st_s = sb("st_s", [P, HP, DB, HD])
        ws_t = sb("ws_t", [P, AHEADS, CH])
        z_rows = sb("z_rows", [2 + 2 * DB, BW], F32, place["ws_t"])
        ws_s = sb("ws_s", [NS, AHEADS, NS])
        bs = sb("bs", [P, 2, CH])
        ln = sb("ln", [P, 2, AW])
        probs_s = sb("probs_s", [NS, HEADS, NS], F32, place["ln"])
        bn = sb("bn", [P, NC + 1, 6])
        mv = sb("mv", [P, NC + 1, 2])
        rstd = sb("rstd", [P, NC + 1])
        assert max(at[0], ffn_end) <= nc.sbuf_usable_end, (at[0], ffn_end, nc.sbuf_usable_end)
        at[0] = mix0
        xrow = sb("xrow", [P, NC + 1, D])

        ident = cst[:, C_ID:C_ID + P]
        ps = ctx.enter_context(nc.psum_tensor("ps", [P, 8, 512], F32))

        def sem(name):
            return ctx.enter_context(nc.semaphore(name))

        def signal(name, per=0):
            return Signal(sem(name), per)

        w_landed = [sem(f"w_landed{s}") for s in range(RING)]
        w_hi_made = [sem(f"w_hi_made{s}") for s in range(RING)]
        w_lo_made = [sem(f"w_lo_made{s}") for s in range(RING)]
        w_used = [sem(f"w_used{s}") for s in range(RING)]
        x_landed, const_landed = sem("x_landed"), sem("const_landed")
        eps_set = sem("eps_set")
        waits_carried = sem("waits_carried")
        turned_in, turned_in_out = sem("turned_in"), sem("turned_in_out")
        prm_turned, x_ready = sem("prm_turned"), sem("x_ready")
        final_turned, final_out = sem("final_turned"), sem("final_out")
        mix_free = sem("mix_free")
        tables_landed = signal("tables_landed", 16 * 13)
        z_zeroed = signal("z_zeroed", 1)
        stored = signal("stored", 16 * 12)
        prm_ready = signal("prm_ready", 1)
        h_hi_made = signal("h_hi_made", 2 * 16)
        h_lo_made = signal("h_lo_made", 2 * 16)
        pre_sq = signal("pre_sq", 2 * 8)
        pre_acc = signal("pre_acc", 2 * 6)
        pre_sum = signal("pre_sum", 2 * 2)
        pre_root = signal("pre_root", 2 * 2)
        r_pre_made = signal("r_pre_made", 2 * 2)
        post_sq = signal("post_sq", 2 * 8)
        post_acc = signal("post_acc", 2 * 6)
        y_made = signal("y_made", 2 * 16)
        post_sum = signal("post_sum", 2 * 2)
        post_root = signal("post_root", 2 * 2)
        r_post_made = signal("r_post_made", 2 * 2)
        x_updated = signal("x_updated", 2 * 8)
        win_done, win_out = signal("win_done", N_WIN // 2), signal("win_out", N_WIN)
        wide_done = signal("wide_done", 8)
        gate_done, gate_out = signal("gate_done", 11), signal("gate_out", 22)
        up_done, up_out = signal("up_done", 11), signal("up_out", 22)
        silu_made, f_made = signal("silu_made", 22), signal("f_made", 22)
        f_hi_made, f_lo_made = signal("f_hi_made", 22), signal("f_lo_made", 22)
        mix_pe = signal("mix_pe", len(TASK))
        swapped = signal("swapped", 4)
        roped = signal("roped", 4)
        v_tok_made, k_tok_made = signal("v_tok_made", 5), signal("k_tok_made", 5)
        spatial_made, setup_read = signal("spatial_made", 1), signal("setup_read", 1)
        probs_made, q_decayed, state_made = signal("probs_made", 5), signal("q_decayed", 4), signal("state_made", 4)
        o_made, o_squared, o_rooted = signal("o_made", 5), signal("o_squared", 5), signal("o_rooted", 5)
        o_normed = signal("o_normed", 5)
        ln_stats, ln_rooted = signal("ln_stats", 2), signal("ln_rooted", 2)
        vn_read, vn_made = signal("vn_read", 2), signal("vn_made", 2)
        mixed_read, a_made = signal("mixed_read", 2), signal("a_made", 2)
        z_made, z_last_made, z_rows_made = signal("z_made", 1), signal("z_last_made", 1), signal("z_rows_made", 1)
        b_made = signal("b_made", 1)
        ab_hi_made, ab_lo_made = signal("ab_hi_made", 2), signal("ab_lo_made", 2)
        values_spread, sample_state = signal("values_spread", 2), signal("sample_state", 4)
        silu_g = signal("silu_g", 2)
        c_made, c_hi_made, c_lo_made = signal("c_made", 2), signal("c_hi_made", 2), signal("c_lo_made", 2)
        y_stored = signal("y_stored")
        vec_own = Own(sem("vec_own"), VEC_OWN)

        block = ctx.enter_context(nc.Block())

        def cols(half):
            return slice(H2 * half, H2 * half + H2)

        def bank_pair(group, half):
            return ps[:, 4 * group + 2 * half:4 * group + 2 * half + 2, 0:H2]

        def square_room(half, pair):
            if pair == 0:
                return acc[:, :, cols(half)]
            e, h = [((1, 0), (0, 0), (1, 1)), ((0, 1), (1, 0), (0, 0))][half][pair - 1]
            return E[e][:, :, cols(h)]

        def alone(eng):
            eng.sem_inc(waits_carried, 1)

        def pair_done(eng, layer, half, done, n, pos, more=0):
            if half == 0:
                eng.wait_ge(done.sem, done.at(layer, n))
            else:
                eng.wait_ge(w_used[pos % RING], USES[pos % RING] * layer + pos // RING + more + 2)

        def over(ap, shape):
            return ap.to_broadcast(shape)

        @block.sync
        def _(sp):
            def load(layer, pos, more, src, nk=4):
                s = pos % RING
                sp.wait_ge(w_used[s], USES[s] * layer + pos // RING + more + 1)
                alone(sp)
                sp.dma_start(w_raw[s][:, 0:nk, :], src).then_inc(w_landed[s], 16)

            def part(w, layer, k0, nk, c0):
                rows = w[bass.ds(layer, 1), P * k0:P * (k0 + nk), bass.ds(c0, 256)]
                return rows.rearrange("o (k p) c -> p (o k) c", p=P)

            with sp.Fori(0, DEPTH) as l:
                for i, c in enumerate(WIN_COLUMNS):
                    for kh in range(2):
                        load(l, 2 * i + kh, 0, part(w_in, l, 4 * kh, 4, 256 * c))
                for n, (c, kh) in enumerate(OUT_ORDER):
                    load(l, OUT0 + n, 0, part(w_out, l, 4 * kh, 4, 256 * c))
                with sp.Fori(0, FT // 2) as j:
                    for i, w in enumerate((w_gate, w_up)):
                        for kh in range(2):
                            load(l, FFN0 + 2 * i + kh, j, part(w, l, 4 * kh, 4, j * 256))
                for n, (c, k0, nk) in enumerate(DOWN):
                    load(l, DOWN0 + n, 0, part(w_down, l, k0, nk, 256 * c), nk)

        @block.gpsimd
        def _(pool):
            pool.memset(ones[:], 1.0).then_inc(eps_set, 1)
            pool.memset(eps[:], EPS).then_inc(eps_set, 1)
            pool.dma_start(cst[:], const).then_inc(const_landed, 16)
            for l in range(DEPTH):
                for i, g in enumerate((g_pre_mix, g_post_mix, g_pre_ffn, g_post_ffn)):
                    pool.dma_start(prow[NPRM * l + 8 * i:NPRM * l + 8 * i + 8, :],
                                   g[l].rearrange("(t p) -> t p", p=P)).then_inc(const_landed, 16)
                pool.dma_start(prow[NPRM * l + CONV:NPRM * l + CONV + 6, :],
                               conv_w[l].rearrange("w (t p) -> (w t) p", p=P)).then_inc(const_landed, 16)
            with pool.Fori(0, DEPTH) as l:
                one = bass.ds(l, 1)
                pool.wait_ge(mix_free, l + 1)
                alone(pool)
                pool.memset(z_p[:, :, 0:2], 0.0).then_inc(z_zeroed.sem, 1)

                def table_in(dst, src):
                    pool.dma_start(dst, src).then_inc(tables_landed.sem, 16)

                table_in(tab[:], table)
                table_in(bs_row[:], b_s[one].rearrange("o h i -> (o h) i"))
                table_in(ln_row[:, 0, :], ln_g[one])
                table_in(ln_row[:, 1, :], ln_b[one])
                for h in range(AHEADS):
                    table_in(ws_in[:, h, :], w_s[one, h].rearrange("o i j -> (o i) j"))
                table_in(sc_in[:], state_conv[one].rearrange("o b w c -> (o b w) c"))
                for hp in range(HP):
                    table_in(st_s[:, hp], state_ret[one, :, 2 * hp:2 * hp + 2]
                             .rearrange("o b h d e -> (h d) (o b) e"))

                def store(dst, src):
                    pool.dma_start(dst, src).then_inc(stored.sem, 16)

                pool.wait_ge(vn_made.sem, vn_made.at(l, 2))
                alone(pool)
                store(chunkv_sample[one].rearrange("o b t h d -> (o b t) (h d)"), vn[0:NS, NC, :])
                pool.wait_ge(z_rows_made.sem, z_rows_made.at(l, 1))
                alone(pool)
                store(conv_prompt[one].rearrange("o b w c -> (o b w) c"), z_rows[0:2, :])
                store(conv_sample[one].rearrange("o b w c -> (o b w) c"), z_rows[2:2 + 2 * DB, :])
                pool.wait_ge(state_made.sem, state_made.at(l, NC))
                alone(pool)
                store(ret_prompt[one, 0].rearrange("o (q h) d e -> (h d) (o q) e", h=2), st_p[:])
                for r in range(2):
                    pool.wait_ge(sample_state.sem, sample_state.at(l, 2 * r + 2))
                    alone(pool)
                    for hp in range(2 * r, 2 * r + 2):
                        for e in range(2):
                            b0 = 4 * e
                            store(ret_sample[one, b0:b0 + 4, 2 * hp:2 * hp + 2]
                                  .rearrange("o b h d e -> (h d) (o b) e"), st_s[:, hp, b0:b0 + 4])
                pool.wait_ge(stored.sem, stored.at(l + 1, 0))

        @block.tensor
        def _(pe):
            for s in range(RING):
                pe.sem_inc(w_used[s], 1)
            transpose = nc.tensor.transpose

            def unit_half(layer, pos, more, ks, source, group, half, first, last, done=None,
                          tile_ready=lambda k: None, after_two=lambda: None):
                s = pos % RING
                if half == 0:
                    pe.wait_ge(w_hi_made[s], USES[s] * layer + pos // RING + more + 1)
                    pe.wait_ge(w_lo_made[s], USES[s] * layer + pos // RING + more + 1)
                for i, k in enumerate(ks):
                    if i == 2:
                        after_two()
                    tile_ready(k)
                    hi, lo = source(k)
                    begins, ends = first and i == 0, last and i == len(ks) - 1
                    for ct in range(2):
                        out = ps[:, 4 * group + 2 * half + ct, 0:H2]
                        wh, wl = (w[s][:, i, P * ct:P * ct + P] for w in (w_hi, w_lo))
                        pe.matmul(out, wh, hi[:, cols(half)], start=begins, stop=False)
                        pe.matmul(out, wl, hi[:, cols(half)], start=False, stop=False)
                        mm = pe.matmul(out, wh, lo[:, cols(half)], start=False, stop=ends)
                if half:
                    mm.then_inc(w_used[s], 1)
                elif done is not None:
                    mm.then_inc(done.sem, 1)

            def unit(layer, pos, more, ks, source, group, first, last, done=None, before_half=lambda half: None):
                for half in range(2):
                    before_half(half)
                    unit_half(layer, pos, more, ks, source, group, half, first, last, done)

            def from_h(k):
                return h_hi[:, k, :], h_lo[:, k, :]

            def from_mix(k):
                if k < 2:
                    return ab_hi[:, k, :], a_lo[:, k, :]
                if k < 4:
                    return ab_hi[:, k, :], b_lo[:, k - 2, :]
                return c_hi[:, k - 4, :], c_lo[:, k - 4, :]

            def from_f(k):
                return f_hi[:, k, :], f_lo[:, k, :]

            def sum_squares(layer, squares, n, sums, bank, half):
                pe.wait_ge(squares.sem, squares.at(layer, n))
                for ct in range(2):
                    mm = pe.matmul(ps[:, bank, 0:H2], ones[:], acc[:, ct, cols(half)],
                                   start=(ct == 0), stop=(ct == 1))
                mm.then_inc(sums.sem, 1)

            def normed_units(layer, norm, pos, dones, out, sum_last=lambda: None):
                for half in range(2):
                    for i in range(4):
                        def h_ready(k):
                            n = 16 * norm + 8 * half + k + 1
                            pe.wait_ge(h_hi_made.sem, h_hi_made.at(layer, n))
                            pe.wait_ge(h_lo_made.sem, h_lo_made.at(layer, n))
                        if half and i == 2:
                            pe.wait_ge(pre_root.sem, pre_root.at(layer, 2 * norm + 1))
                        kh = i % 2
                        unit_half(layer, pos + i, 0, range(4 * kh, 4 * kh + 4), from_h, i // 2, half, kh == 0, kh == 1,
                                  dones[i // 2] if kh else None, h_ready if i < 2 else (lambda k: None))
                        if half == 0 and i == 1:
                            sum_last()
                        if half == 0 and i == 2:
                            sum_squares(layer, pre_acc, 6 * norm + 3, pre_sum, 6, 0)
                pe.wait_ge(*out)
                sum_squares(layer, pre_acc, 6 * norm + 6, pre_sum, 0, 1)
                pe.wait_ge(pre_root.sem, pre_root.at(layer, 2 * norm + 2))

            pe.wait_ge(eps_set, 2)
            pe.wait_ge(const_landed, 16 * 11)
            transpose(ps[:, 0, 0:2 * NPRM], prow[:], ident[0:2 * NPRM, 0:2 * NPRM]).then_inc(prm_turned, 1)
            pe.wait_ge(x_landed, 32)
            for k in range(KT):
                if k >= 2:
                    pe.wait_ge(turned_in_out, k - 1)
                for c in range(NC):
                    transpose(ps[:, 4 + k % 2, P * c:P * c + P], xrow[:, c, P * k:P * k + P], ident)
                transpose(ps[:, 6 + k % 2, 0:NS], xrow[0:NS, NC, P * k:P * k + P],
                          ident[0:NS, 0:NS]).then_inc(turned_in, 1)

            with pe.Fori(0, DEPTH) as l:
                task = [0]

                def task_done(ins):
                    ins.then_inc(mix_pe.sem, 1)
                    task[0] += 1

                def after(signal, n):
                    pe.wait_ge(signal.sem, signal.at(l, n))

                def setup_weights():
                    pe.wait_ge(tables_landed.sem, tables_landed.at(l, 16 * 13))
                    pe.wait_ge(win_out.sem, win_out.at(l, 4))
                    pe.matmul(ps[:, 5, 0:512], ones[0:1, :], ln_row[:].rearrange("p a c -> p (a c)"),
                              start=True, stop=True)
                    for h in range(AHEADS):
                        tr = transpose(ps[:, 4, P * h:P * h + P], ws_in[:, h, :], ident)
                    task_done(tr)

                def setup_rows():
                    after(spatial_made, 1)
                    for hp in range(2):
                        pe.matmul(ps[:, 7, CH * hp:CH * hp + CH], cst[0:AHEADS, C_SEL + P * hp:C_SEL + P * hp + P],
                                  bs_row[:], start=True, stop=True)
                        transpose(ps[:, 7, 256 + 2 * DB * hp:256 + 2 * DB * (hp + 1)],
                                  sc_in[:, P * hp:P * hp + P], ident[0:2 * DB, 0:2 * DB])
                    first = ws_t[0:DS, :, 0:DS].rearrange("p h (o t) -> p h o t", o=1)
                    task_done(pe.matmul(ps[0:NS, 6, 0:AHEADS * NS].rearrange("p (h b t) -> p h b t", h=AHEADS, t=DS),
                                        cst[0:DS, C_REP:C_REP + NS], over(first, [DS, AHEADS, DB, DS]),
                                        start=True, stop=True))

                def turn(src, bank, dst_c, rows_bank, free):
                    free()
                    for c in range(NC):
                        transpose(ps[:, bank, P * c:P * c + P], src[:, P * c:P * c + P], ident)
                    task_done(transpose(ps[0:NS, rows_bank, dst_c:dst_c + P], src[:, SEQ:T], ident))

                def turn_k(hp):
                    def free():
                        pe.wait_ge(roped.sem, roped.at(l, hp // 2 + 1))
                        after(*((k_tok_made, hp - 1) if hp >= 2 else (setup_read, 1)))
                    turn(kT[:, hp, :], 4 + hp % 2, P * hp, 6, free)

                def turn_v(hp):
                    def free():
                        pe.wait_ge(win_out.sem, win_out.at(l, 2 * (V01 + hp // 2) + 2))
                        if hp >= 2:
                            after(v_tok_made, hp - 1)
                        else:
                            after(k_tok_made, hp + 3)
                    turn(E[(V01 + hp // 2) % 2][:, hp % 2, :], 4 + hp % 2, P * hp, 7, free)

                def turn_av():
                    pe.wait_ge(win_out.sem, win_out.at(l, 2 * AV + 2))
                    after(v_tok_made, 5)
                    after(k_tok_made, 5)
                    for c in range(NC):
                        for ct in range(2):
                            tr = transpose(ps[:, 6 + c // 2, 256 * (c % 2) + P * ct:256 * (c % 2) + P * ct + P],
                                           E[AV % 2][:, ct, P * c:P * c + P], ident)
                    task_done(tr)

                def turn_av_s():
                    after(probs_made, 1)
                    for ct in range(2):
                        tr = transpose(ps[0:NS, 4, P * ct:P * ct + P], E[AV % 2][:, ct, SEQ:T], ident)
                    task_done(tr)

                def scores(c):
                    for h in range(HEADS):
                        rows = slice(HD * (h % 2), HD * (h % 2) + HD)
                        mm = pe.matmul(ps[:, 4 + h % 2, P * (h // 2):P * (h // 2) + P],
                                       kT[rows, h // 2, P * c:P * c + P], qo[rows, h // 2, P * c:P * c + P],
                                       start=True, stop=True)
                    return mm

                def attend(c):
                    after(probs_made, c + 1)
                    if c == 0:
                        after(v_tok_made, 5)
                        after(vn_read, 1)
                    else:
                        after(q_decayed, c)
                        after(state_made, c)
                        after(o_made, c)
                        after(o_rooted, c)
                    for h in range(HEADS):
                        rows = slice(HD * (h % 2), HD * (h % 2) + HD)
                        out = ps[rows, 6, P * (h // 2):P * (h // 2) + P]
                        pe.matmul(out, v_tok[:, c, HD * h:HD * h + HD], probs[:, c % 2, by_parity(h), :],
                                  start=True, stop=(c == 0))
                        if c:
                            pe.matmul(out, st_p[rows, h // 2, :], qd[rows, h // 2, :], start=False, stop=True)
                    for h in range(HEADS):
                        rows = slice(HD * (h % 2), HD * (h % 2) + HD)
                        mm = pe.matmul(ps[rows, 7, HD * (h // 2):HD * (h // 2) + HD],
                                       k_tok[:, c, HD * h:HD * h + HD], v_tok[:, c, HD * h:HD * h + HD],
                                       start=True, stop=True)
                    return mm

                def norm_o(c):
                    n = HP * CH if c < NC else HP * NS
                    after(o_squared, c + 1)
                    after(state_made, min(c + 1, NC))
                    if c == NC:
                        after(o_rooted, NC)
                    task_done(pe.matmul(ps[:, 7, 0:n], cst[:, C_BLK:C_BLK + P],
                                        rn[:, c % 2].rearrange("p q i -> p (q i)")[:, 0:n], start=True, stop=True))

                def scores_s():
                    for h in range(HEADS):
                        rows = slice(HD * (h % 2), HD * (h % 2) + HD)
                        mm = pe.matmul(ps[0:NS, 4 + h % 2, NS * (h // 2):NS * (h // 2) + NS], kT[rows, h // 2, SEQ:T],
                                       qo[rows, h // 2, SEQ:T], start=True, stop=True)
                    return mm

                def attend_s():
                    after(probs_made, 5)
                    after(o_made, 4)
                    for h in range(HEADS):
                        rows = slice(HD * (h % 2), HD * (h % 2) + HD)
                        base = NS * (h // 2)
                        pe.matmul(ps[rows, 6, base:base + NS], v_tok[0:NS, NC, HD * h:HD * h + HD],
                                  probs_s[:, by_parity(h), :], start=True, stop=False, skip_group_check=True)
                        for b in range(DB):
                            pe.matmul(ps[rows, 6, base + DS * b:base + DS * b + DS], st_s[rows, h // 2, b, :],
                                      qds[rows, h // 2, DS * b:DS * b + DS], start=False, stop=(b == DB - 1),
                                      skip_group_check=True)
                    after(z_last_made, 1)
                    after(probs_made, 5)
                    for ct in range(2):
                        tr = transpose(ps[0:2 + 2 * DB, 5, P * ct:P * ct + P], z_last[:, ct, :], ident)
                    task_done(tr)

                def state_s(r, banks):
                    after(values_spread, r + 1)
                    for i, hp in enumerate((2 * r, 2 * r + 1)):
                        for e in range(2):
                            h = 2 * hp + e
                            mm = pe.matmul(ps[HD * e:HD * e + HD, banks[i], 0:512],
                                           k_tok[0:NS, NC, HD * h:HD * h + HD],
                                           vexp[:, 2 * i + e].rearrange("p b e -> p (b e)"),
                                           start=True, stop=True)
                    task_done(mm)

                def mix_tokens():
                    after(probs_made, 2)
                    after(vn_made, 2)
                    for h in range(AHEADS):
                        for c in range(NC):
                            mm = pe.matmul(ps[HD * (h % 2):HD * (h % 2) + HD, 4 + h // 2, P * c:P * c + P],
                                           vn[:, c, HD * h:HD * h + HD], ws_t[:, h, :], start=True, stop=True)
                    task_done(mm)

                def mix_tokens_s():
                    after(probs_made, 3)
                    alone(pe)
                    for h in range(AHEADS):
                        mm = pe.matmul(ps[HD * (h % 2):HD * (h % 2) + HD, 4, NS * (h // 2):NS * (h // 2) + NS],
                                       vn[0:NS, NC, HD * h:HD * h + HD], ws_s[:, h, :], start=True, stop=True)
                    task_done(mm)

                def first_scores():
                    pe.wait_ge(roped.sem, roped.at(l, 4))
                    after(v_tok_made, 4)
                    task_done(scores(0))

                def chunk_step(c):
                    def run():
                        attend(c)
                        if c == 0:
                            after(vn_read, 2)
                        elif c == 1:
                            after(mixed_read, 1)
                        elif c == 2:
                            after(mixed_read, 2)
                        if c < NC - 1:
                            task_done(scores(c + 1))
                        else:
                            after(probs_made, 4)
                            alone(pe)
                            task_done(scores_s())
                    return run

                tasks = {"setup_weights": setup_weights, "setup_rows": setup_rows, "scores0": first_scores,
                         "turn_av": turn_av, "turn_av_s": turn_av_s, "mix_tokens": mix_tokens,
                         "mix_tokens_s": mix_tokens_s, "attend_s": attend_s,
                         "state_s0": lambda: state_s(0, (4, 5)), "state_s1": lambda: state_s(1, (6, 7))}
                for n in range(4):
                    tasks[f"turn_k{n}"] = lambda n=n: turn_k(n)
                    tasks[f"turn_v{n}"] = lambda n=n: turn_v(n)
                    tasks[f"chunk{n}"] = chunk_step(n)
                for n in range(NC + 1):
                    tasks[f"norm_o{n}"] = lambda n=n: norm_o(n)

                for u in range(N_WIN):
                    pair, kh = u // 2, u % 2

                    def before(half, u=u, pair=pair, kh=kh):
                        if kh == 0:
                            pe.wait_ge(win_out.sem, win_out.at(l, 2 * (pair - 1) + half + 1) if pair > 2
                                       else win_out.at(l, half + 1))
                    if u == 0:
                        normed_units(l, 0, 0, (win_done, win_done), (win_out.sem, win_out.at(l, 1)))
                    elif u >= 4:
                        unit(l, u, 0, range(4 * kh, 4 * kh + 4), from_h, 0, kh == 0, kh == 1,
                             win_done if kh else None, before)
                    for name in TASKS_AFTER.get(u, []):
                        tasks[name]()
                        assert task[0] == TASK[name]

                for n, (pair, kh) in enumerate(OUT_ORDER):
                    def before(half, pair=pair, kh=kh):
                        if kh == 0:
                            pe.wait_ge(post_sq.sem, post_sq.at(l, 2 * pair + half) + 1)
                    if n == 0:
                        pe.wait_ge(win_out.sem, win_out.at(l, N_WIN))
                        after(ab_hi_made, 2)
                        after(ab_lo_made, 2)
                    if n == 1:
                        after(sample_state, 4)
                        after(o_rooted, 5)
                    if n == 2:
                        after(c_hi_made, 2)
                        after(c_lo_made, 2)
                    if pair < 3:
                        unit(l, OUT0 + n, 0, range(4 * kh, 4 * kh + 4), from_mix, pair % 2,
                             kh == 0, kh == 1, wide_done if kh else None, before)

                def post_sums(norm, half):
                    sum_squares(l, post_acc, 6 * norm + 5 + half, post_sum, 2 + half, half)

                for half in range(2):
                    pe.wait_ge(post_sq.sem, post_sq.at(l, 6 + half) + 1)
                    for n in (6, 7):
                        kh = n - 6
                        unit_half(l, OUT0 + n, 0, range(4 * kh, 4 * kh + 4), from_mix, 1, half, kh == 0, kh == 1,
                                  wide_done if kh else None,
                                  after_two=(lambda: post_sums(0, 0)) if half and kh == 0 else (lambda: None))

                def ffn_pair(j):
                    for i, (done, out) in enumerate(((gate_done, gate_out), (up_done, up_out))):
                        for kh in range(2):
                            def before(half, kh=kh, out=out):
                                if kh == 0:
                                    pe.wait_ge(out.sem, out.at(l, j * 2 + half + 1))
                            unit(l, FFN0 + 2 * i + kh, j, range(4 * kh, 4 * kh + 4), from_h, i,
                                 kh == 0, kh == 1, done if kh else None, before)
                normed_units(l, 1, FFN0, (gate_done, up_done), (gate_out.sem, gate_out.at(l, 3)),
                             lambda: post_sums(0, 1))
                alone(pe)
                with pe.Fori(1, FT // 2) as j:
                    ffn_pair(j)

                def down_half(n, half, after_two=lambda: None):
                    pair, k0, nk = DOWN[n]
                    g = pair % 2
                    if k0 == 0:
                        pe.wait_ge(post_sq.sem, post_sq.at(l, 8 + 2 * pair + half) + 1)
                    if pair == 0 and half == 0:
                        pe.wait_ge(f_lo_made.sem, f_lo_made.at(l, min(22, k0 + 4)))
                    if pair < 2 and k0 == 0 and half == 0:
                        out = up_out if g else gate_out
                        pe.wait_ge(out.sem, out.at(l, 24))
                    ends = k0 + nk == FT
                    unit_half(l, DOWN0 + n, 0, range(k0, k0 + nk), from_f, g, half, k0 == 0, ends,
                              wide_done if ends else None, after_two=after_two)
                for n in range(N_DOWN - DOWN_TAIL):
                    for half in range(2):
                        down_half(n, half)
                for half in range(2):
                    for n in range(N_DOWN - DOWN_TAIL, N_DOWN):
                        down_half(n, half, (lambda: post_sums(1, 0)) if half and n == N_DOWN - DOWN_TAIL
                                  else (lambda: None))
                post_sums(1, 1)

            pe.wait_ge(x_updated.sem, x_updated.at(DEPTH, 0))
            pe.wait_ge(r_post_made.sem, r_post_made.at(DEPTH, 0))
            for n in range(2 * (NC + 1)):
                c, kq = n // 2, n % 2
                m = P if c < NC else NS
                if n >= 8:
                    pe.wait_ge(final_out, n - 7)
                for k in range(4):
                    tr = transpose(ps[0:m, n % 8, P * k:P * k + P], x[:, 4 * kq + k, P * c:P * c + m], ident)
                tr.then_inc(final_turned, 1)

        @block.scalar
        def _(act):
            act.dma_start(xrow[:, 0:NC, :], x_prompt[0].rearrange("(c p) d -> p c d", p=P)).then_inc(x_landed, 16)
            act.dma_start(xrow[0:NS, NC, :], x_sample.rearrange("b t d -> (b t) d")).then_inc(x_landed, 16)
            act.sem_inc(post_sq.sem, 4)

            def split(layer, pos, more=0, nk=4):
                s = pos % RING
                act.wait_ge(w_landed[s], (USES[s] * layer + pos // RING + more + 1) * 16)
                act.activation(w_hi[s][:, 0:nk, :], w_raw[s][:, 0:nk, :], ACT.Copy).then_inc(w_hi_made[s], 1)

            for k in range(KT):
                act.wait_ge(turned_in, k + 1)
                act.activation(x[:, k, 0:SEQ], ps[:, 4 + k % 2, :], ACT.Copy)
                act.activation(x[:, k, SEQ:T], ps[:, 6 + k % 2, 0:NS], ACT.Copy).then_inc(turned_in_out, 1)

            with act.Fori(0, DEPTH) as l:

                def after(signal, n):
                    act.wait_ge(signal.sem, signal.at(l, n))

                def pre_half(norm, gain, half, updated, pos):
                    for pair in range(4):
                        updated(pair)
                        for ct in range(2):
                            k = 2 * pair + ct
                            act.activation(h_hi[:, k, cols(half)], x[:, k, cols(half)], ACT.Copy,
                                           scale=prm[:, gain + k:gain + k + 1]).then_inc(h_hi_made.sem, 1)
                        if half == 0 and pair == 2:
                            split(l, pos + 2)
                        if half and pair >= 2:
                            act.wait_ge(pre_acc.sem, pre_acc.at(l, 6 * norm + pair - 1))
                        act.activation(square_room(half, pair), x[:, 2 * pair:2 * pair + 2, cols(half)],
                                       ACT.Square).then_inc(pre_sq.sem, 1)
                    if half == 0:
                        split(l, pos + 3)

                def pre_root_half(norm, half):
                    act.wait_ge(pre_sum.sem, pre_sum.at(l, 2 * norm + half + 1))
                    act.activation(r_pre[:, 0, cols(half)], ps[:, 6 - 6 * half, 0:H2], ACT.Sqrt,
                                   bias=eps[:, 0:1], scale=1.0 / D).then_inc(pre_root.sem, 1)

                def post_half(norm, pair, gain, pos, half):
                    group = pair % 2
                    pair_done(act, l, half, wide_done, 4 * norm + pair + 1, pos)
                    if pair == 0 and norm and half == 0:
                        after(f_lo_made, 22)
                    if pair >= 2:
                        act.wait_ge(post_acc.sem, post_acc.at(l, 6 * norm + 2 * (pair - 2) + half + 1))
                    squares = acc if pair == 0 else E[0]
                    for ct in range(2):
                        k = 2 * pair + ct
                        act.activation(y[:, k, cols(half)], ps[:, 4 * group + 2 * half + ct, 0:H2], ACT.Copy,
                                       scale=prm[:, gain + k:gain + k + 1]).then_inc(y_made.sem, 1)
                    act.activation(squares[:, :, cols(half)], bank_pair(group, half), ACT.Square)\
                       .then_inc(post_sq.sem, 1)

                def post_root_half(norm, half):
                    act.wait_ge(post_sum.sem, post_sum.at(l, 2 * norm + half + 1))
                    act.activation(r_post[:, 0, cols(half)], ps[:, 2 + half, 0:H2], ACT.Sqrt,
                                   bias=eps[:, 0:1], scale=1.0 / D).then_inc(post_root.sem, 1)

                split(l, 0)
                split(l, 1)
                act.wait_ge(prm_ready.sem, prm_ready.at(l, 1))
                act.wait_ge(eps_set, 2)
                for half in range(2):
                    act.wait_ge(x_ready, 2 * l + half + 1)
                    pre_half(0, G_PRE_MIX, half, lambda pair: None, 0)

                def swap(pair, n):
                    act.wait_ge(win_out.sem, win_out.at(l, 2 * pair + 2))
                    if n:
                        act.wait_ge(roped.sem, roped.at(l, n))
                    for qd_ in range(4):
                        to = 32 * (qd_ ^ 1)
                        ins = act.activation(acc[to:to + 32], E[pair % 2][32 * qd_:32 * qd_ + 32], ACT.Copy)
                    ins.then_inc(swapped.sem, 1)

                def v_tok_out(hp):
                    after(mix_pe, TASK[f"turn_v{hp}"])
                    act.activation(v_tok[:, 0:NC, P * hp:P * hp + P],
                                   ps[:, 4 + hp % 2, :].rearrange("p (c f) -> p c f", c=NC), ACT.Copy)\
                       .then_inc(v_tok_made.sem, 1)
                    if hp == HP - 1:
                        act.activation(v_tok[0:NS, NC, :], ps[0:NS, 7, :], ACT.Copy).then_inc(v_tok_made.sem, 1)

                def o_out(c):
                    after(mix_pe, TASK[f"chunk{c}" if c < NC else "attend_s"])
                    m = CH if c < NC else NS
                    o = ps[:, 6, 0:HP * m].rearrange("p (q i) -> p q i", q=HP)
                    if c >= 2:
                        after(o_normed, c - 1)
                    squares = rn[:, c % 2].rearrange("p q i -> p (q i)")[:, 0:HP * m]
                    act.activation(squares, ps[:, 6, 0:HP * m], ACT.Square).then_inc(o_squared.sem, 1)
                    if c:
                        after(q_decayed, c)
                    act.activation(qo[:, :, CH * c:CH * c + m], o, ACT.Copy).then_inc(o_made.sem, 1)

                def o_root(c):
                    after(mix_pe, TASK[f"norm_o{c}"])
                    n = HP * (CH if c < NC else NS)
                    act.activation(rn[:, c % 2].rearrange("p q i -> p (q i)")[:, 0:n], ps[:, 7, 0:n], ACT.Sqrt,
                                   bias=eps[:, 0:1]).then_inc(o_rooted.sem, 1)

                def ln_root(m, chunks, n):
                    after(ln_stats, n)
                    act.activation(rstd[0:m, chunks], mv[0:m, chunks, 1], ACT.Sqrt, bias=eps[0:m, 0:1])\
                       .then_inc(ln_rooted.sem, 1)

                for u in range(2, N_WIN):
                    if u == 2:
                        pre_root_half(0, 0)
                    split(l, u + LEAD)
                    pair, kh = u // 2, u % 2
                    if u == 3:
                        pre_root_half(0, 1)
                        swap(K01, 0)
                    if u == 4:
                        swap(K23, 1)
                    if kh and pair in (Q01, Q23):
                        swap(pair, pair - Q01 + 2)
                    for hp in range(HP):
                        if f"turn_v{hp}" in TASKS_AFTER.get(u, []):
                            v_tok_out(hp)
                    if u == 14:
                        ln_root(P, slice(0, NC), 1)
                    if u == 15:
                        ln_root(NS, slice(NC, NC + 1), 2)
                    if u in (16, 18, 20, 22):
                        o_out((u - 16) // 2)
                    if u in (17, 19, 21, 23):
                        o_root((u - 17) // 2)
                    if u == 20:
                        after(a_made, 2)
                        act.activation(ab_hi[:, 0:2, :], a_u[:], ACT.Copy).then_inc(ab_hi_made.sem, 1)
                    if u == 21:
                        after(z_made, 1)
                        act.activation(z_last[:, :, 0:2], z_p[:, :, SEQ:SEQ + 2], ACT.Copy)
                        for ct in range(2):
                            ins = act.activation(z_last[:, ct, 2:].rearrange("p (b w) -> p b w", w=2),
                                                 z_s[:, ct, :, DS:DS + 2], ACT.Copy)
                        ins.then_inc(z_last_made.sem, 1)
                    if u == 23:
                        o_out(NC)
                        after(b_made, 1)
                        act.activation(ab_hi[:, 2:4, :], b_b[:], ACT.Copy).then_inc(ab_hi_made.sem, 1)
                    if u == 24:
                        o_root(NC)
                    if kh and pair in (G01, G23):
                        act.wait_ge(win_out.sem, win_out.at(l, 2 * pair + 2))
                        act.activation(sg[:, 2 * (pair - G01):2 * (pair - G01) + 2, :],
                                                       E[pair % 2][:], ACT.Silu).then_inc(silu_g.sem, 1)
                for i in range(2):
                    after(c_made, i + 1)
                    act.activation(c_hi[:, 2 * i:2 * i + 2, :], qo[:, 2 * i:2 * i + 2, :], ACT.Copy).then_inc(c_hi_made.sem, 1)

                for n in range(N_WOUT):
                    split(l, OUT0 + n + LEAD)
                    if n in OUT_LAST:
                        for half in range(2):
                            post_half(0, OUT_LAST[n], G_POST_MIX, OUT0 + n, half)
                            if n == N_WOUT - 1 and half == 0:
                                post_root_half(0, 0)
                for half in range(2):
                    if half:
                        post_root_half(0, 1)
                    pre_half(1, G_PRE_FFN, half,
                             lambda pair: act.wait_ge(x_updated.sem, x_updated.at(l, 4 * half + pair + 1)), FFN0)

                def ffn_pair(j, first):
                    if first:
                        pre_root_half(1, 0)
                    else:
                        split(l, FFN0 + 2, j)
                        split(l, FFN0 + 3, j)
                    if first:
                        split(l, FFN0 + 4, j)
                        split(l, FFN0 + 5, j)
                        pre_root_half(1, 1)
                    for half in range(2):
                        act.wait_ge(gate_out.sem, gate_out.at(l, j * 2 + half + 1 + 2))
                        act.activation(E[1][:, :, cols(half)], E[0][:, :, cols(half)], ACT.Silu)\
                           .then_inc(silu_made.sem, 1)
                    if not first:
                        split(l, FFN0 + 4, j)
                        split(l, FFN0 + 5, j)
                    for half in range(2):
                        act.wait_ge(f_made.sem, f_made.at(l, j * 2 + half + 1))
                        act.activation(f_hi[:, bass.ds(j * 2, 2), cols(half)], acc[:, :, cols(half)], ACT.Copy)\
                           .then_inc(f_hi_made.sem, 1)
                after(stored, stored.per)
                ffn_pair(0, True)
                with act.Fori(1, FT // 2) as j:
                    ffn_pair(j, False)

                for n, (pair, k0, nk) in enumerate(DOWN):
                    if n + LEAD < N_DOWN:
                        split(l, DOWN0 + n + LEAD, nk=DOWN[n + LEAD][2])
                    if k0 + nk == FT:
                        for half in range(2):
                            post_half(1, pair, G_POST_FFN, DOWN0 + n, half)
                            if pair == 3:
                                post_root_half(1, half)

            act.wait_ge(stored.sem, stored.at(DEPTH, 0))
            for n in range(2 * (NC + 1)):
                c, kq = n // 2, n % 2
                m = P if c < NC else NS
                act.wait_ge(final_turned, n + 1)
                act.activation(xrow[0:m, c, 512 * kq:512 * kq + 512], ps[0:m, n % 8, :], ACT.Copy)\
                   .then_inc(final_out, 1)
                if kq:
                    act.wait_ge(final_out, n + 1)
                    dst = y_prompt[0, P * c:P * c + P, :] if c < NC else y_sample.rearrange("b t d -> (b t) d")
                    act.dma_start(dst, xrow[0:m, c, :]).then_inc(y_stored.sem, 16)
            act.wait_ge(y_stored.sem, 16 * (NC + 1))

        @block.vector
        def _(vec):
            vec.sem_inc(gate_out.sem, 2)
            vec.sem_inc(up_out.sem, 2)

            def split(layer, pos, more=0, nk=4):
                s = pos % RING
                vec.wait_ge(w_hi_made[s], USES[s] * layer + pos // RING + more + 1)
                vec.tensor_tensor(w_lo[s][:, 0:nk, :], w_raw[s][:, 0:nk, :], w_hi[s][:, 0:nk, :], ALU.subtract)\
                   .then_inc(w_lo_made[s], 1)

            vec.wait_ge(prm_turned, 1)
            vec.tensor_copy(prm_all[:].rearrange("p l n -> p (l n)"), ps[:, 0, 0:2 * NPRM]).then_inc(prm_turned, 1)
            vec.wait_ge(turned_in_out, KT)
            vec.sem_inc(x_ready, 2)
            vec.sem_inc(mix_free, 1)

            with vec.Fori(0, DEPTH) as l:
                vec_own.n = 0

                def after(signal, n):
                    vec.wait_ge(signal.sem, signal.at(l, n))

                def then(ins):
                    after(vec_own, vec_own.mark(ins))

                def low_tiles(norm, gain, half, pair):
                    for k in (2 * pair, 2 * pair + 1):
                        vec.wait_ge(h_hi_made.sem, h_hi_made.at(l, 16 * norm + 8 * half + k + 1))
                        vec.scalar_tensor_tensor(h_lo[:, k, cols(half)], x[:, k, cols(half)],
                                                 prm[:, gain + k:gain + k + 1], h_hi[:, k, cols(half)],
                                                 ALU.mult, ALU.subtract).then_inc(h_lo_made.sem, 1)

                def add_squares(norm, half):
                    for pair in range(1, 4):
                        n = 6 * norm + 3 * half + pair
                        vec.wait_ge(pre_sq.sem, pre_sq.at(l, 8 * norm + 4 * half + pair + 1))
                        if pair > 1:
                            vec.wait_ge(pre_acc.sem, pre_acc.at(l, n - 1))
                        vec.tensor_tensor(acc[:, :, cols(half)], acc[:, :, cols(half)],
                                          square_room(half, pair), ALU.add).then_inc(pre_acc.sem, 1)

                def recip_pre(norm, half):
                    vec.wait_ge(pre_root.sem, pre_root.at(l, 2 * norm + half + 1))
                    vec.reciprocal(r_pre[:, 0, cols(half)], r_pre[:, 0, cols(half)]).then_inc(r_pre_made.sem, 1)
                    vec.wait_ge(r_pre_made.sem, r_pre_made.at(l, 2 * norm + half + 1))

                def scaled_out(dst, group, half, out, done, n, pos, more=0):
                    pair_done(vec, l, half, done, n, pos, more)
                    vec.tensor_tensor(dst[:, :, cols(half)], bank_pair(group, half),
                                      over(r_pre[:, :, cols(half)], [P, 2, H2]), ALU.mult).then_inc(out.sem, 1)

                def post_add(norm, pair, half):
                    n = 6 * norm + 2 * (pair - 1) + half
                    vec.wait_ge(post_sq.sem, post_sq.at(l, 8 * norm + 2 * pair + half + 1) + 4)
                    if pair > 1:
                        vec.wait_ge(post_acc.sem, post_acc.at(l, n - 1))
                    vec.tensor_tensor(acc[:, :, cols(half)], acc[:, :, cols(half)], E[0][:, :, cols(half)],
                                      ALU.add).then_inc(post_acc.sem, 1)

                def recip_post(norm, half):
                    vec.wait_ge(post_root.sem, post_root.at(l, 2 * norm + half + 1))
                    vec.reciprocal(r_post[:, 0, cols(half)], r_post[:, 0, cols(half)]).then_inc(r_post_made.sem, 1)
                    vec.wait_ge(r_post_made.sem, r_post_made.at(l, 2 * norm + half + 1))
                    vec.wait_ge(y_made.sem, y_made.at(l, 16 * norm + 14 + 2 * half))

                def update(half, pair):
                    yy = y[:, 2 * pair:2 * pair + 2, cols(half)]
                    xx = x[:, 2 * pair:2 * pair + 2, cols(half)]
                    then(vec.tensor_tensor(yy, yy, over(r_post[:, :, cols(half)], [P, 2, H2]), ALU.mult))
                    vec.tensor_tensor(xx, xx, yy, ALU.add).then_inc(x_updated.sem, 1)

                vec.wait_ge(prm_turned, 2)
                vec.tensor_copy(prm[:], prm_all[:, bass.ds(l, 1), :].rearrange("p o n -> p (o n)"))\
                   .then_inc(prm_ready.sem, 1)
                split(l, 0)
                split(l, 1)
                for half in range(2):
                    for pair in range(4):
                        low_tiles(0, G_PRE_MIX, half, pair)
                        if half == 0 and pair == 2:
                            split(l, 2)
                    if half == 0:
                        split(l, 3)
                    add_squares(0, half)

                def rope(pair, n, dst):
                    hp = 2 * (n % 2)
                    cos = over(tab[:, T_COS:T_COS + T].rearrange("p (o t) -> p o t", o=1), [P, 2, T])
                    sin = over(tab[:, T_SIN:T_SIN + T].rearrange("p (o t) -> p o t", o=1), [P, 2, T])
                    out = dst[:, hp:hp + 2, :]
                    vec.tensor_tensor(out, E[pair % 2][:], cos, ALU.mult)
                    vec.wait_ge(swapped.sem, swapped.at(l, n + 1))
                    then(vec.tensor_tensor(acc[:], acc[:], sin, ALU.mult))
                    vec.tensor_tensor(out, out, acc[:], ALU.add).then_inc(roped.sem, 1)

                def k_tok_out(hp):
                    after(mix_pe, TASK[f"turn_k{hp}"])
                    kdec = cst[:, C_KDEC + 2 * hp:C_KDEC + 2 * hp + 2]
                    for e in range(2):
                        ins = vec.tensor_scalar(
                            k_tok[:, 0:NC, P * hp + HD * e:P * hp + HD * e + HD],
                            ps[:, 4 + hp % 2, :].rearrange("p (c f) -> p c f", c=NC)[:, :, HD * e:HD * e + HD],
                            kdec[:, e:e + 1], None, ALU.mult)
                    ins.then_inc(k_tok_made.sem, 1)
                    if hp == HP - 1:
                        vec.tensor_tensor(
                            k_tok[0:NS, NC, :].rearrange("p (h d) -> p h d", h=HEADS),
                            ps[0:NS, 6, :].rearrange("p (h d) -> p h d", h=HEADS),
                            over(cst[0:NS, C_KDECS:C_KDECS + HEADS].rearrange("p (h o) -> p h o", o=1),
                                 [NS, HEADS, HD]), ALU.mult).then_inc(k_tok_made.sem, 1)

                def probs_out(c):
                    after(mix_pe, TASK[f"chunk{c - 1}" if c else "scores0"])
                    vec.tensor_tensor(probs[:, c % 2].rearrange("p h i -> p (h i)"),
                                           ps[:, 4:6, :].rearrange("p b i -> p (b i)"),
                                           tab[:, T_DM:T_DM + 1024], ALU.mult).then_inc(probs_made.sem, 1)

                def q_decay(c):
                    qdec = tab[:, T_QD:T_QD + 640].rearrange("p (q i) -> p q i", q=HP)
                    vec.tensor_tensor(qd[:], qo[:, :, P * c:P * c + P], qdec[:, :, 0:CH], ALU.mult).then_inc(q_decayed.sem, 1)

                def state_out(c):
                    upd = ps[:, 7, 0:HP * HD].rearrange("p (q e) -> p q e", q=HP)
                    if c == 0:
                        vec.tensor_copy(st_p[:], upd).then_inc(state_made.sem, 1)
                        return
                    dec = over(cst[:, C_CDEC:C_CDEC + HP].rearrange("p (q o) -> p q o", o=1), [P, HP, HD])
                    then(vec.tensor_tensor(st_p[:], st_p[:], dec, ALU.mult))
                    vec.tensor_tensor(st_p[:], st_p[:], upd, ALU.add).then_inc(state_made.sem, 1)

                def o_norm(c):
                    m = CH if c < NC else NS
                    r = rn[:, c % 2].rearrange("p q i -> p (q i)")[:, 0:HP * m]
                    oo = qo[:, :, CH * c:CH * c + m]
                    after(o_rooted, c + 1)
                    then(vec.reciprocal(r, r))
                    vec.tensor_tensor(oo, oo, r.rearrange("p (q i) -> p q i", q=HP), ALU.mult)\
                       .then_inc(o_normed.sem, 1)

                def layer_norm(chunks, src, m, n):
                    for c in chunks:
                        ins = vec.bn_stats(bn[0:m, c, :], src(c))
                    n_own = vec_own.mark(ins)
                    after(vec_own, n_own)
                    alone(vec)
                    for c in chunks:
                        ins = vec.bn_aggr(mv[0:m, c, :], bn[0:m, c, :])
                    ins.then_inc(ln_stats.sem, 1)
                    part = slice(chunks[0], chunks[-1] + 1)
                    after(ln_rooted, n)
                    then(vec.reciprocal(rstd[0:m, part], rstd[0:m, part]))
                    for c in chunks:
                        ins = vec.tensor_scalar(vn[0:m, c, :], src(c), mv[0:m, c, 0:1], rstd[0:m, c:c + 1],
                                                ALU.subtract, ALU.mult)
                    ins.then_inc(vn_read.sem, 1)
                    after(vn_read, n)
                    shape = [m, len(chunks), AW]
                    then(vec.tensor_tensor(vn[0:m, part, :], vn[0:m, part, :], over(ln[0:m, 0:1, :], shape), ALU.mult))
                    vec.tensor_tensor(vn[0:m, part, :], vn[0:m, part, :], over(ln[0:m, 1:2, :], shape), ALU.add)\
                       .then_inc(vn_made.sem, 1)

                for u in range(2, N_WIN):
                    pair, kh = u // 2, u % 2
                    if u == 3:
                        recip_pre(0, 1)
                        scaled_out(E[K01], 0, 1, win_out, win_done, 1, 1)
                    split(l, u + LEAD)
                    if u == 2:
                        recip_pre(0, 0)
                        scaled_out(E[K01], 0, 0, win_out, win_done, 1, 1)
                    if u == 3:
                        for half in range(2):
                            scaled_out(E[K23], 1, half, win_out, win_done, 2, 3)
                        vec.wait_ge(win_out.sem, win_out.at(l, 4))
                        vec.wait_ge(tables_landed.sem, tables_landed.at(l, 16 * 13))
                        rope(K01, 0, kT)
                    elif kh:
                        if pair in (V01, V23):
                            vec.wait_ge(swapped.sem, swapped.at(l, pair - V01 + 1))
                        if pair in (Q01, Q23):
                            after(mix_pe, TASK["turn_v1" if pair == Q01 else "turn_v3"])
                        if pair == AV:
                            vec.wait_ge(swapped.sem, swapped.at(l, 3))
                        if pair == BC:
                            vec.wait_ge(swapped.sem, swapped.at(l, 4))
                        if pair == BX:
                            after(mix_pe, TASK["turn_av_s"])
                        dst = {AU: a_u, BB: b_b}.get(pair, E[pair % 2])
                        for half in range(2):
                            scaled_out(dst, 0, half, win_out, win_done, pair + 1, 2 * pair + 1)
                        vec.wait_ge(win_out.sem, win_out.at(l, 2 * pair + 2))
                    if u == 4:
                        rope(K23, 1, kT)
                        vec.wait_ge(z_zeroed.sem, z_zeroed.at(l, 1))
                        after(mix_pe, TASK["setup_weights"])
                        vec.tensor_tensor(ws_t[:], ps[:, 4, :].rearrange("p (h i) -> p h i", h=AHEADS),
                                               over(tab[:, T_TRIL:T_TRIL + P].rearrange("p (o i) -> p o i", o=1),
                                                    [P, AHEADS, CH]), ALU.mult).then_inc(spatial_made.sem, 1)
                        vec.tensor_copy(ln[:].rearrange("p a c -> p (a c)"), ps[:, 5, :])
                        after(mix_pe, TASK["setup_rows"])
                        vec.tensor_copy(bs[:].rearrange("p a c -> p (a c)"), ps[:, 7, 0:256])
                        for ct in range(2):
                            vec.tensor_copy(z_s[:, ct, :, 0:2],
                                            ps[:, 7, 256 + 2 * DB * ct:256 + 2 * DB * (ct + 1)]
                                            .rearrange("p (b w) -> p b w", w=2))
                        vec.tensor_tensor(ws_s[:], ps[0:NS, 6, 0:NS * AHEADS].rearrange("p (h i) -> p h i", h=AHEADS),
                                               over(tab[0:NS, T_TRILS:T_TRILS + NS].rearrange("p (o i) -> p o i", o=1),
                                                    [NS, AHEADS, NS]), ALU.mult).then_inc(setup_read.sem, 1)
                        after(setup_read, 1)
                    if kh and pair in (Q01, Q23):
                        rope(pair, pair - Q01 + 2, qo)
                    for hp in range(HP):
                        if f"turn_k{hp}" in TASKS_AFTER.get(u, []):
                            k_tok_out(hp)
                    if u == 13:
                        probs_out(0)
                    if u == 14:
                        after(mix_pe, TASK["turn_av"])
                        layer_norm(range(NC), lambda c: ps[:, 6 + c // 2, 256 * (c % 2):256 * (c % 2) + 256], P, 1)
                    if u == 15:
                        after(mix_pe, TASK["turn_av_s"])
                        layer_norm(range(NC, NC + 1), lambda c: ps[0:NS, 4, 0:AW], NS, 2)
                    if u in (16, 18, 20):
                        c = (u - 16) // 2
                        probs_out(c + 1)
                        q_decay(c + 1)
                        state_out(c)
                    if u in (17, 19, 21, 23):
                        o_norm((u - 17) // 2)
                    if u == 17:
                        after(mix_pe, TASK["mix_tokens"])
                        mixed = ps[:, 4:6, :].rearrange("p h (c i) -> p h c i", c=NC)
                        for hp in range(2):
                            ins = vec.tensor_tensor(E[1][:, hp, 0:SEQ].rearrange("p (c i) -> p c i", c=NC),
                                                    mixed[:, hp], over(bs[:, hp:hp + 1, :], [P, NC, CH]), ALU.add)
                        ins.then_inc(mixed_read.sem, 1)
                        after(mixed_read, 1)
                        vec.tensor_tensor(a_u[:, :, 0:SEQ], a_u[:, :, 0:SEQ], E[1][:, :, 0:SEQ], ALU.mult).then_inc(a_made.sem, 1)
                    if u == 19:
                        after(mix_pe, TASK["mix_tokens_s"])
                        for hp in range(2):
                            ins = vec.tensor_tensor(E[0][:, hp, 0:NS].rearrange("p (b t) -> p b t", t=DS),
                                                    ps[:, 4, NS * hp:NS * hp + NS].rearrange("p (b t) -> p b t", t=DS),
                                                    over(bs[:, hp:hp + 1, 0:DS], [P, DB, DS]), ALU.add)
                        ins.then_inc(mixed_read.sem, 1)
                        after(mixed_read, 2)
                        vec.tensor_tensor(a_u[:, :, SEQ:T], a_u[:, :, SEQ:T], E[0][:, :, 0:NS], ALU.mult).then_inc(a_made.sem, 1)
                    if u == 21:
                        zi = [E[BC % 2], E[BX % 2]]
                        vec.tensor_tensor(z_p[:, :, 2:], zi[0][:, :, 0:SEQ], zi[1][:, :, 0:SEQ], ALU.mult)
                        for ct in range(2):
                            ins = vec.tensor_tensor(z_s[:, ct, :, 2:],
                                                    zi[0][:, ct, SEQ:T].rearrange("p (b t) -> p b t", t=DS),
                                                    zi[1][:, ct, SEQ:T].rearrange("p (b t) -> p b t", t=DS), ALU.mult)
                        ins.then_inc(z_made.sem, 1)
                        after(z_made, 1)
                        out = E[BC % 2]
                        for tap in range(3):
                            for ct in range(2):
                                w = prm[:, CONV + 2 * tap + ct:CONV + 2 * tap + ct + 1]
                                pairs = ((out[:, ct, 0:SEQ], z_p[:, ct, tap:tap + SEQ]),
                                         (out[:, ct, SEQ:T].rearrange("p (b t) -> p b t", t=DS),
                                          z_s[:, ct, :, tap:tap + DS]))
                                for o, z in pairs:
                                    if tap == 0:
                                        ins = vec.tensor_scalar(o, z, w, None, ALU.mult)
                                    else:
                                        ins = vec.scalar_tensor_tensor(o, z, w, o, ALU.mult, ALU.add)
                            then(ins)
                        vec.tensor_tensor(b_b[:], b_b[:], out[:], ALU.mult).then_inc(b_made.sem, 1)
                        after(ab_hi_made, 1)
                        vec.tensor_tensor(a_lo[:], a_u[:], ab_hi[:, 0:2, :], ALU.subtract).then_inc(ab_lo_made.sem, 1)
                        qdec = tab[:, T_QD:T_QD + 640].rearrange("p (q i) -> p q i", q=HP)
                        vec.tensor_tensor(qds[:], qo[:, :, SEQ:T], qdec[:, :, CH:CH + NS], ALU.mult).then_inc(q_decayed.sem, 1)
                    if u == 22:
                        after(mix_pe, TASK["chunk3"])
                        state_out(3)
                        vec.tensor_tensor(probs_s[:].rearrange("p (e q) i -> p e (q i)", e=2), ps[0:NS, 4:6, 0:HP * NS],
                                          tab[0:NS, T_DMS:T_DMS + 256].rearrange("p (e r) -> p e r", e=2), ALU.mult).then_inc(probs_made.sem, 1)

                    def expand(r):
                        for i in range(4):
                            h = 4 * r + i
                            v = v_tok[0:NS, NC, HD * h:HD * h + HD].rearrange("p (o e) -> p o e", o=1)
                            m = cst[0:NS, C_BMASK:C_BMASK + DB].rearrange("p (b o) -> p b o", o=1)
                            ins = vec.tensor_tensor(vexp[:, i], over(v, [NS, DB, HD]), over(m, [NS, DB, HD]), ALU.mult)
                        ins.then_inc(values_spread.sem, 1)

                    def state_s_out(r, banks):
                        for i, hp in enumerate((2 * r, 2 * r + 1)):
                            ins = vec.scalar_tensor_tensor(
                                st_s[:, hp].rearrange("p b e -> p (b e)"), st_s[:, hp].rearrange("p b e -> p (b e)"),
                                cst[:, C_CDECS + hp:C_CDECS + hp + 1], ps[:, banks[i], 0:512], ALU.mult, ALU.add)
                            ins.then_inc(sample_state.sem, 1)

                    if u == 23:
                        after(mix_pe, TASK["attend_s"])
                        vec.tensor_copy(z_rows[:], ps[0:2 + 2 * DB, 5, 0:BW]).then_inc(z_rows_made.sem, 1)
                        expand(0)
                        after(ab_hi_made, 2)
                        vec.tensor_tensor(b_lo[:], b_b[:], ab_hi[:, 2:4, :], ALU.subtract).then_inc(ab_lo_made.sem, 1)
                    if u == 24:
                        o_norm(NC)
                        after(mix_pe, TASK["state_s0"])
                        expand(1)
                        state_s_out(0, (4, 5))
                    if u == 25:
                        after(mix_pe, TASK["state_s1"])
                        state_s_out(1, (6, 7))
                for i in range(2):
                    after(silu_g, i + 1)
                    oo = qo[:, 2 * i:2 * i + 2, :]
                    vec.tensor_tensor(oo, oo, sg[:, 2 * i:2 * i + 2, :], ALU.mult).then_inc(c_made.sem, 1)
                for i in range(2):
                    after(c_hi_made, i + 1)
                    vec.tensor_tensor(c_lo[:, 2 * i:2 * i + 2, :], qo[:, 2 * i:2 * i + 2, :],
                                      c_hi[:, 2 * i:2 * i + 2, :], ALU.subtract).then_inc(c_lo_made.sem, 1)

                for n in range(N_WOUT):
                    split(l, OUT0 + n + LEAD)
                    if OUT_LAST.get(n, 0) in (1, 2):
                        for half in range(2):
                            post_add(0, OUT_LAST[n], half)
                for half in range(2):
                    if half == 0:
                        post_add(0, 3, 0)
                    recip_post(0, half)
                    for pair in range(4):
                        update(half, pair)
                        if pair:
                            low_tiles(1, G_PRE_FFN, half, pair - 1)
                        if half == 0 and pair == 3:
                            split(l, FFN0 + 2)
                    low_tiles(1, G_PRE_FFN, half, 3)
                    if half == 0:
                        post_add(0, 3, 1)
                        split(l, FFN0 + 3)
                    add_squares(1, half)

                def ffn_pair(j, first):
                    if first:
                        recip_pre(1, 0)
                        scaled_out(E[0], 0, 0, gate_out, gate_done, j + 1, FFN0 + 1, j)
                        split(l, FFN0 + 4, j)
                        split(l, FFN0 + 5, j)
                        recip_pre(1, 1)
                        scaled_out(E[0], 0, 1, gate_out, gate_done, j + 1, FFN0 + 1, j)
                    else:
                        split(l, FFN0 + 2, j)
                        split(l, FFN0 + 3, j)
                        for half in range(2):
                            scaled_out(E[0], 0, half, gate_out, gate_done, j + 1, FFN0 + 1, j)
                        split(l, FFN0 + 4, j)
                        split(l, FFN0 + 5, j)
                    for half in range(2):
                        scaled_out(acc, 1, half, up_out, up_done, j + 1, FFN0 + 3, j)
                        vec.wait_ge(silu_made.sem, silu_made.at(l, j * 2 + half + 1))
                        vec.wait_ge(up_out.sem, up_out.at(l, j * 2 + half + 1 + 2))
                        vec.tensor_tensor(acc[:, :, cols(half)], acc[:, :, cols(half)], E[1][:, :, cols(half)],
                                          ALU.mult).then_inc(f_made.sem, 1)
                    for half in range(2):
                        vec.wait_ge(f_hi_made.sem, f_hi_made.at(l, j * 2 + half + 1))
                        vec.tensor_tensor(f_lo[:, bass.ds(j * 2, 2), cols(half)], acc[:, :, cols(half)],
                                          f_hi[:, bass.ds(j * 2, 2), cols(half)], ALU.subtract)\
                           .then_inc(f_lo_made.sem, 1)
                after(stored, stored.per)
                ffn_pair(0, True)
                with vec.Fori(1, FT // 2) as j:
                    ffn_pair(j, False)

                for n, (pair, k0, nk) in enumerate(DOWN):
                    if n + LEAD < N_DOWN:
                        split(l, DOWN0 + n + LEAD, nk=DOWN[n + LEAD][2])
                    if k0 + nk == FT:
                        for half in range(2):
                            if pair:
                                post_add(1, pair, half)
                            if pair == 3:
                                recip_post(1, half)
                                for q in range(4):
                                    update(half, q)
                                vec.wait_ge(x_updated.sem, x_updated.at(l, 8 + 4 * half + 4))
                                vec.sem_inc(x_ready, 1)
                vec.sem_inc(mix_free, 1)
                assert vec_own.n == vec_own.per, vec_own.n


_INS = ["x_prompt", "x_sample", "state_ret", "state_conv", "w_in", "w_out", "w_s", "b_s", "ln_g", "ln_b", "conv_w",
        "g_pre_mix", "g_post_mix", "g_pre_ffn", "g_post_ffn", "w_gate", "w_up", "w_down"]
_OUTS = [(1, SEQ, D), (DB, DS, D), (DEPTH, 1, HEADS, HD, HD), (DEPTH, DB, HEADS, HD, HD),
         (DEPTH, 1, 2, BW), (DEPTH, DB, 2, BW), (DEPTH, DB, DS, AHEADS, HD)]


def kernel(**inputs):
    import concourse.bacc as bacc
    from concourse.bass_utils import run_bass_kernel_spmd

    nc = bacc.Bacc("TRN2", target_bir_lowering=False, num_devices=1)
    named = {n: np.ascontiguousarray(inputs[n]) for n in _INS}
    named["const"], named["table"] = tables()
    arrays, args = {}, []
    for name, a in named.items():
        arrays[f"in_{name}"] = a
        args.append(nc.dram_tensor(f"in_{name}", a.shape, mybir.dt.from_np(a.dtype), kind="ExternalInput").ap())
    for i, shape in enumerate(_OUTS):
        args.append(nc.dram_tensor(f"out_{i}", shape, F32, kind="ExternalOutput").ap())
    build(nc, *args)
    r = run_bass_kernel_spmd(nc, [arrays], core_ids=[0])
    return tuple(r.results[0][f"out_{i}"] for i in range(len(_OUTS)))
```

```python
from contextlib import ExitStack

import numpy as np

import concourse.bass as bass
from concourse import mybir

F32 = mybir.dt.float32
F32R = mybir.dt.float32r
ACT = mybir.ActivationFunctionType
ALU = mybir.AluOpType

P = 128
DEPTH, D, FF = 2, 1024, 2816
SEQ, DB, DS = 512, 8, 4
NS = DB * DS
T = SEQ + NS
H2 = T // 2
CH = 128
NC = SEQ // CH
FIRST_CHUNKS = -(-H2 // CH)
HEADS, HD, AHEADS = 8, 64, 4
HP = HEADS // 2
AW = BW = 256
KT = D // P
FT = FF // P
EPS = 1e-6

K01, K23, V01, V23, Q01, Q23, AV, AU, BB, BC, BX, G01, G23 = range(13)
WIN_COLUMNS = [7, 8, 9, 10, 5, 6, 1, 0, 2, 3, 4, 11, 12]
N_WIN = 2 * len(WIN_COLUMNS)
N_WOUT = 8
N_FFN = 4 * (FF // 256)
DOWN = [(pair, sum(ks[:i]), nk)
        for pair, ks in enumerate(3 * [[4, 4, 4, 4, 4, 2]] + [[2, 2, 2, 2, 4, 4, 4, 2]])
        for i, nk in enumerate(ks)]
DOWN_TAIL = 3
N_DOWN = len(DOWN)
OUT0, FFN0, DOWN0 = N_WIN, N_WIN + N_WOUT, N_WIN + N_WOUT + N_FFN
UNITS = DOWN0 + N_DOWN
RING = 4
USES = [sum(1 for u in range(UNITS) if u % RING == s) for s in range(RING)]
LEAD = 2

TASKS_AFTER = {
    4: ["setup_weights"], 5: ["setup_rows"], 6: ["turn_k0", "turn_k1"], 7: ["turn_k2", "turn_k3"],
    8: ["turn_v0", "turn_v1"], 9: ["turn_v2"], 10: ["turn_v3"], 13: ["scores0"], 14: ["turn_av"],
    15: ["turn_av_s"], 16: ["chunk0"], 17: ["mix_tokens", "norm_o0"], 18: ["chunk1"],
    19: ["mix_tokens_s", "norm_o1"], 20: ["chunk2"], 21: ["norm_o2"], 22: ["chunk3"],
    23: ["attend_s", "norm_o3"], 24: ["norm_o4", "state_s0"], 25: ["state_s1"],
}
TASK = {name: n + 1 for n, name in enumerate(t for ts in TASKS_AFTER.values() for t in ts)}
OUT_ORDER = [(0, 0), (1, 0), (0, 1), (1, 1), (2, 0), (2, 1), (3, 0), (3, 1)]
OUTPUTS = [(0, 0), (0, 1), (1, 0), (1, 1), (2, 0), (3, 0), (NC, 0), (2, 1), (3, 1), (NC, 1)]
BY_SCALAR, BY_VECTOR = [0, 1, 2, 3, 4, 5, 6, 8], [7, 9]
OUT_LAST = {2: 0, 3: 1, 5: 2, 7: 3}

G_PRE_MIX, G_POST_MIX, G_PRE_FFN, G_POST_FFN, CONV = 0, 8, 16, 24, 32
NPRM = 38

C_ID, C_BLK, C_CDEC, C_CDECS, C_KDEC, C_KDECS, C_BMASK, C_REP, C_SEL = 0, 128, 256, 260, 264, 272, 280, 288, 320
N_CONST = 576
T_DM, T_DMS, T_COS, T_SIN, T_QD, T_QDS, T_TRIL, T_TRILS = 0, 1024, 1280, 1824, 2368, 2880, 2912, 3040
N_TAB = 3072


def tables():
    f = np.float32
    log_g = np.log(1.0 - 2.0 ** (-5.0 - np.arange(HEADS)))
    scale = HD ** -0.5
    c = np.zeros((P, N_CONST), f)
    c[:, C_ID:C_ID + P] = np.eye(P)
    c[:, C_BLK:C_BLK + P] = np.kron(np.eye(2), np.full((HD, HD), 1.0 / HD))
    part_head = np.arange(P) // HD
    for hp in range(HP):
        c[:, C_CDEC + hp] = np.exp(log_g[2 * hp + part_head] * CH)
        c[:, C_CDECS + hp] = np.exp(log_g[2 * hp + part_head] * DS)
    j = np.arange(P)
    js = np.arange(NS)
    c[:, C_KDEC:C_KDEC + HEADS] = np.exp(log_g[None] * (CH - 1 - j)[:, None])
    c[:NS, C_KDECS:C_KDECS + HEADS] = np.exp(log_g[None] * (DS - 1 - js % DS)[:, None])
    c[:NS, C_BMASK:C_BMASK + DB] = js[:, None] // DS == np.arange(DB)[None]
    c[:DS, C_REP:C_REP + NS] = np.arange(DS)[:, None] == js[None] % DS
    for hp in range(2):
        for h in range(AHEADS):
            c[h, C_SEL + P * hp:C_SEL + P * (hp + 1)] = part_head + 2 * hp == h
    t = np.zeros((P, N_TAB), f)
    diff = j[None] - j[:, None]
    dm = np.where(diff[None] >= 0, np.exp(log_g[:, None, None] * np.maximum(diff, 0)[None]), 0) * scale
    order = sorted(range(HEADS), key=by_parity)
    t[:, T_DM:T_DM + 1024] = dm[order].transpose(1, 0, 2).reshape(P, -1)
    ds_ = js[None] - js[:, None]
    same = (js[None] // DS == js[:, None] // DS) & (ds_ >= 0)
    dms = np.where(same[None], np.exp(log_g[:, None, None] * np.maximum(ds_, 0)[None]), 0) * scale
    t[:NS, T_DMS:T_DMS + 256] = dms[order].transpose(1, 0, 2).reshape(NS, -1)
    half = HD // 2
    inv = (10000.0 ** (-np.arange(half) / half)).astype(f)
    pos = np.concatenate([np.arange(SEQ), np.tile(4096 + np.arange(DS), DB)]).astype(f)
    ang = (pos[None] * inv[j % half][:, None]).astype(f)
    sign = np.where((j // half) % 2 == 0, -1.0, 1.0)[:, None]
    t[:, T_COS:T_COS + T] = np.cos(ang)
    t[:, T_SIN:T_SIN + T] = np.sin(ang) * sign
    for hp in range(HP):
        dec = np.exp(log_g[2 * hp + part_head][:, None] * (j + 1.0)[None]) * scale
        t[:, T_QD + CH * hp:T_QD + CH * (hp + 1)] = dec
        for e in range(2):
            t[:, T_QDS + DS * (2 * hp + e):T_QDS + DS * (2 * hp + e + 1)] = dec[:, :DS] * (part_head == e)[:, None]
    t[:, T_TRIL:T_TRIL + P] = diff >= 0
    t[:NS, T_TRILS:T_TRILS + NS] = same
    return c, t


def by_parity(h):
    return 4 * (h % 2) + h // 2


class Signal:

    def __init__(self, sem, per_layer):
        self.sem, self.per, self.n = sem, per_layer, 0

    def at(self, layer, n):
        return layer * self.per + n


VEC_OWN = 37


class Own(Signal):

    def mark(self, ins):
        ins.then_inc(self.sem, 1)
        self.n += 1
        return self.n


def build(nc, x_prompt, x_sample, state_ret, state_conv, w_in, w_out, w_s, b_s, ln_g, ln_b, conv_w,
          g_pre_mix, g_post_mix, g_pre_ffn, g_post_ffn, w_gate, w_up, w_down, const, table,
          y_prompt, y_sample, ret_prompt, ret_sample, conv_prompt, conv_sample, chunkv_sample):
    ctx = ExitStack()
    with ctx:
        at = [(nc.sbuf_base + 31) // 32 * 32]

        def sb(name, shape, dt=F32, where=None):
            size = 4 * int(np.prod(shape[1:]))
            if where is None:
                where = at[0]
                at[0] += (size + 31) // 32 * 32
            buf = nc.alloc_sbuf_tensor_at(name, shape, dt, offset=where)
            place[name] = where
            return buf

        place = {}
        cst = sb("cst", [P, N_CONST])
        x = sb("x", [P, KT, T])
        prm_all = sb("prm_all", [P, DEPTH * NPRM])
        prm = sb("prm", [P, NPRM])
        prow = sb("prow", [2 * NPRM, P])
        eps = sb("eps", [P, 1])
        spare = sb("spare", [P, 1])
        ones = sb("ones", [P, P])
        r_pre = sb("r_pre", [P, 1, T])
        r_post = sb("r_post", [P, 1, T])
        acc = sb("acc", [P, 2, T])
        E = [sb(f"evac{i}", [P, 2, T]) for i in range(2)]
        h_hi = sb("h_hi", [P, KT, T], F32R)
        h_lo = sb("h_lo", [P, KT, T], F32R)
        y = sb("y", [P, KT, T], F32, place["h_hi"])
        w_raw = [sb(f"w_raw{s}", [P, 4, 256]) for s in range(RING)]
        w_hi = [sb(f"w_hi{s}", [P, 4, 256], F32R) for s in range(RING)]
        w_lo = [sb(f"w_lo{s}", [P, 4, 256], F32R, place[f"w_raw{s}"]) for s in range(RING)]
        mix0 = at[0]
        f_hi = sb("f_hi", [P, FT, T], F32R)
        f_lo = sb("f_lo", [P, FT, T], F32R)
        ffn_end = at[0]
        at[0] = mix0
        tab = sb("tab", [P, N_TAB])
        v_tok = sb("v_tok", [P, NC + 1, 512])
        k_tok = sb("k_tok", [P, NC + 1, 512])
        qo = sb("qo", [P, HP, T])
        c_lo = sb("c_lo", [P, HP, T], F32R, place["qo"])
        kT = sb("kT", [P, HP, T])
        qd = sb("qd", [P, HP, CH], F32, place["r_post"])
        rn = sb("rn", [P, 2, HP, CH], F32, place["acc"])
        qds = sb("qds", [P, HP, 2, DB, DS])
        probs = sb("probs", [P, 2, HEADS, CH])
        ws_in = sb("ws_in", [P, AHEADS, CH], F32, place["probs"])
        vexp = sb("vexp", [NS, 4, DB, HD], F32, place["probs"])
        sg = sb("sg", [P, HP, T])
        c_hi = sb("c_hi", [P, HP, T], F32R, place["sg"])
        z_p = sb("z_p", [P, 2, SEQ + 2], F32, place["sg"])
        z_s = sb("z_s", [P, 2, DB, DS + 2], F32, place["sg"] + 4 * 2 * (SEQ + 2) + 16)
        a_u = sb("a_u", [P, 2, T])
        a_lo = sb("a_lo", [P, 2, T], F32R, place["a_u"])
        b_b = sb("b_b", [P, 2, T])
        b_lo = sb("b_lo", [P, 2, T], F32R, place["b_b"])
        ab_hi = sb("ab_hi", [P, 4, T], F32R)
        z_last = sb("z_last", [P, 2, 2 + 2 * DB])
        vn = sb("vn", [P, NC + 1, AW])
        ln_row = sb("ln_row", [1, 2, AW], F32, place["vn"])
        bs_row = sb("bs_row", [AHEADS, P], F32, place["vn"] + 2048)
        sc_in = sb("sc_in", [2 * DB, BW], F32, place["vn"] + 2560)
        st_p = sb("st_p", [P, HP, HD])
        st_s = sb("st_s", [P, HP, DB, HD])
        ws_t = sb("ws_t", [P, AHEADS, CH])
        z_rows = sb("z_rows", [2 + 2 * DB, BW], F32, place["ws_t"])
        ws_s = sb("ws_s", [NS, AHEADS, NS])
        bs = sb("bs", [P, 2, CH])
        ln = sb("ln", [P, 2, AW])
        probs_s = sb("probs_s", [NS, HEADS, NS], F32, place["ln"])
        bn = sb("bn", [P, NC + 1, 6])
        mv = sb("mv", [P, NC + 1, 2])
        rstd = sb("rstd", [P, NC + 1])
        assert max(at[0], ffn_end) <= nc.sbuf_usable_end, (at[0], ffn_end, nc.sbuf_usable_end)
        at[0] = mix0
        xrow = sb("xrow", [P, NC + 1, D])

        ident = cst[:, C_ID:C_ID + P]
        ps = ctx.enter_context(nc.psum_tensor("ps", [P, 8, 512], F32))

        def sem(name):
            return ctx.enter_context(nc.semaphore(name))

        def signal(name, per=0):
            return Signal(sem(name), per)

        w_landed = [sem(f"w_landed{s}") for s in range(RING)]
        w_hi_made = [sem(f"w_hi_made{s}") for s in range(RING)]
        w_lo_made = [sem(f"w_lo_made{s}") for s in range(RING)]
        w_used = [sem(f"w_used{s}") for s in range(RING)]
        x_landed = [sem(f"x_landed{c}") for c in range(NC + 1)]
        const_landed, prm_landed = sem("const_landed"), sem("prm_landed")
        eps_set = sem("eps_set")
        waits_carried = sem("waits_carried")
        turned_in, first_tiles_in, last_tiles_in = sem("turned_in"), sem("first_tiles_in"), sem("last_tiles_in")
        prm_turned, x_ready = sem("prm_turned"), sem("x_ready")
        final_turned, final_out, final_out_vec = sem("final_turned"), sem("final_out"), sem("final_out_vec")
        mix_free = sem("mix_free")
        tables_landed = signal("tables_landed", 16 * 13)
        z_zeroed = signal("z_zeroed", 1)
        stored = signal("stored", 16 * 12)
        prm_ready = signal("prm_ready", 1)
        h_hi_made = signal("h_hi_made", 2 * 16)
        h_lo_made = signal("h_lo_made", 2 * 16)
        pre_sq = signal("pre_sq", 2 * 8)
        pre_acc = signal("pre_acc", 2 * 6)
        pre_sum = signal("pre_sum", 2 * 2)
        pre_root = signal("pre_root", 2 * 2)
        r_pre_made = signal("r_pre_made", 2 * 2)
        post_sq = signal("post_sq", 2 * 8)
        post_acc = signal("post_acc", 2 * 6)
        y_made = signal("y_made", 2 * 16)
        post_sum = signal("post_sum", 2 * 2)
        post_root = signal("post_root", 2 * 2)
        r_post_made = signal("r_post_made", 2 * 2)
        x_updated = signal("x_updated", 2 * 8)
        win_done, win_out = signal("win_done", N_WIN // 2), signal("win_out", N_WIN)
        wide_done = signal("wide_done", 8)
        gate_done, gate_out = signal("gate_done", 11), signal("gate_out", 22)
        up_done, up_out = signal("up_done", 11), signal("up_out", 22)
        silu_made, f_made = signal("silu_made", 22), signal("f_made", 22)
        f_hi_made, f_lo_made = signal("f_hi_made", 22), signal("f_lo_made", 22)
        mix_pe = signal("mix_pe", len(TASK))
        swapped = signal("swapped", 4)
        roped = signal("roped", 4)
        v_tok_made, k_tok_made = signal("v_tok_made", 5), signal("k_tok_made", 5)
        spatial_made, setup_read = signal("spatial_made", 1), signal("setup_read", 1)
        probs_made, q_decayed, state_made = signal("probs_made", 5), signal("q_decayed", 4), signal("state_made", 4)
        o_made, o_squared, o_rooted = signal("o_made", 5), signal("o_squared", 5), signal("o_rooted", 5)
        o_normed = signal("o_normed", 5)
        ln_stats, ln_rooted = signal("ln_stats", 2), signal("ln_rooted", 2)
        vn_read, vn_made = signal("vn_read", 2), signal("vn_made", 2)
        mixed_read, a_made = signal("mixed_read", 2), signal("a_made", 2)
        z_made, z_last_made, z_rows_made = signal("z_made", 1), signal("z_last_made", 1), signal("z_rows_made", 1)
        b_made = signal("b_made", 1)
        ab_hi_made, ab_lo_made = signal("ab_hi_made", 2), signal("ab_lo_made", 2)
        values_spread, sample_state = signal("values_spread", 2), signal("sample_state", 4)
        silu_g = signal("silu_g", 2)
        c_made, c_hi_made, c_lo_made = signal("c_made", 2), signal("c_hi_made", 2), signal("c_lo_made", 2)
        y_stored = signal("y_stored")
        vec_own = Own(sem("vec_own"), VEC_OWN)

        block = ctx.enter_context(nc.Block())

        def cols(half):
            return slice(H2 * half, H2 * half + H2)

        def bank_pair(group, half):
            return ps[:, 4 * group + 2 * half:4 * group + 2 * half + 2, 0:H2]

        def load_chunk(eng, c):
            src = x_prompt[0, P * c:P * c + P, :] if c < NC else x_sample.rearrange("b t d -> (b t) d")
            eng.dma_start(xrow[0:rows_of(c), c, :], src).then_inc(x_landed[c], 16)

        def rows_out(eng, n, copy, done):
            c, kq = OUTPUTS[n]
            eng.wait_ge(final_turned, n + 1)
            copy(xrow[0:rows_of(c), c, 512 * kq:512 * kq + 512], ps[0:rows_of(c), output_bank(n), :])\
               .then_inc(done, 1)

        def output_bank(n):
            return [0, 1, 4, 5, 2, 3, 6, 7][n % 8]

        def turned_x(c, kq, copy):
            m = rows_of(c)
            return copy(x[:, 4 * kq:4 * kq + 4, P * c:P * c + m],
                        ps[:, 2 * (c % NC) + kq, 0:4 * m].rearrange("p (k t) -> p k t", k=4))

        def rows_of(c):
            return P if c < NC else NS

        def square_room(half, pair):
            if pair == 0:
                return acc[:, :, cols(half)]
            e, h = [((1, 0), (0, 0), (1, 1)), ((0, 1), (1, 0), (0, 0))][half][pair - 1]
            return E[e][:, :, cols(h)]

        def alone(eng):
            eng.sem_inc(waits_carried, 1)

        def pair_done(eng, layer, half, done, n, pos, more=0):
            if half == 0:
                eng.wait_ge(done.sem, done.at(layer, n))
            else:
                eng.wait_ge(w_used[pos % RING], USES[pos % RING] * layer + pos // RING + more + 2)

        def over(ap, shape):
            return ap.to_broadcast(shape)

        @block.sync
        def _(sp):
            def load(layer, pos, more, src, nk=4):
                s = pos % RING
                sp.wait_ge(w_used[s], USES[s] * layer + pos // RING + more + 1)
                alone(sp)
                sp.dma_start(w_raw[s][:, 0:nk, :], src).then_inc(w_landed[s], 16)

            def part(w, layer, k0, nk, c0):
                rows = w[bass.ds(layer, 1), P * k0:P * (k0 + nk), bass.ds(c0, 256)]
                return rows.rearrange("o (k p) c -> p (o k) c", p=P)

            sp.dma_start(cst[:], const).then_inc(const_landed, 16)
            for c in (1, 3, NC):
                load_chunk(sp, c)
            sp.wait_ge(x_landed[2], 16)
            with sp.Fori(0, DEPTH) as l:
                for i, c in enumerate(WIN_COLUMNS):
                    for kh in range(2):
                        load(l, 2 * i + kh, 0, part(w_in, l, 4 * kh, 4, 256 * c))
                for n, (c, kh) in enumerate(OUT_ORDER):
                    load(l, OUT0 + n, 0, part(w_out, l, 4 * kh, 4, 256 * c))
                with sp.Fori(0, FT // 2) as j:
                    for i, w in enumerate((w_gate, w_up)):
                        for kh in range(2):
                            load(l, FFN0 + 2 * i + kh, j, part(w, l, 4 * kh, 4, j * 256))
                for n, (c, k0, nk) in enumerate(DOWN):
                    load(l, DOWN0 + n, 0, part(w_down, l, k0, nk, 256 * c), nk)
            for n, (c, kq) in enumerate(OUTPUTS):
                order, done = (BY_SCALAR, final_out) if n in BY_SCALAR else (BY_VECTOR, final_out_vec)
                sp.wait_ge(done, order.index(n) + 1)
                dst = y_prompt[0, P * c:P * c + P, :] if c < NC else y_sample.rearrange("b t d -> (b t) d")
                part_ = slice(512 * kq, 512 * kq + 512)
                sp.dma_start(dst[:, part_], xrow[0:rows_of(c), c, part_]).then_inc(y_stored.sem, 16)
            sp.wait_ge(y_stored.sem, 16 * 2 * (NC + 1))

        @block.gpsimd
        def _(pool):
            pool.memset(ones[:], 1.0).then_inc(eps_set, 1)
            pool.memset(eps[:], EPS).then_inc(eps_set, 1)
            pool.memset(r_post[:, 0, cols(1)], 1.0).then_inc(post_root.sem, 1)
            pool.memset(y[:, :, cols(1)], 0.0).then_inc(post_root.sem, 1)
            with pool.Fori(0, DEPTH) as l:
                one = bass.ds(l, 1)
                pool.wait_ge(mix_free, l + 1)
                alone(pool)
                pool.memset(z_p[:, :, 0:2], 0.0).then_inc(z_zeroed.sem, 1)

                def table_in(dst, src):
                    pool.dma_start(dst, src).then_inc(tables_landed.sem, 16)

                table_in(tab[:], table)
                table_in(bs_row[:], b_s[one].rearrange("o h i -> (o h) i"))
                table_in(ln_row[:, 0, :], ln_g[one])
                table_in(ln_row[:, 1, :], ln_b[one])
                for h in range(AHEADS):
                    table_in(ws_in[:, h, :], w_s[one, h].rearrange("o i j -> (o i) j"))
                table_in(sc_in[:], state_conv[one].rearrange("o b w c -> (o b w) c"))
                for hp in range(HP):
                    table_in(st_s[:, hp], state_ret[one, :, 2 * hp:2 * hp + 2]
                             .rearrange("o b h d e -> (h d) (o b) e"))

                def store(dst, src):
                    pool.dma_start(dst, src).then_inc(stored.sem, 16)

                pool.wait_ge(vn_made.sem, vn_made.at(l, 2))
                alone(pool)
                store(chunkv_sample[one].rearrange("o b t h d -> (o b t) (h d)"), vn[0:NS, NC, :])
                pool.wait_ge(z_rows_made.sem, z_rows_made.at(l, 1))
                alone(pool)
                store(conv_prompt[one].rearrange("o b w c -> (o b w) c"), z_rows[0:2, :])
                store(conv_sample[one].rearrange("o b w c -> (o b w) c"), z_rows[2:2 + 2 * DB, :])
                pool.wait_ge(state_made.sem, state_made.at(l, NC))
                alone(pool)
                store(ret_prompt[one, 0].rearrange("o (q h) d e -> (h d) (o q) e", h=2), st_p[:])
                for r in range(2):
                    pool.wait_ge(sample_state.sem, sample_state.at(l, 2 * r + 2))
                    alone(pool)
                    for hp in range(2 * r, 2 * r + 2):
                        for e in range(2):
                            b0 = 4 * e
                            store(ret_sample[one, b0:b0 + 4, 2 * hp:2 * hp + 2]
                                  .rearrange("o b h d e -> (h d) (o b) e"), st_s[:, hp, b0:b0 + 4])
                pool.wait_ge(stored.sem, stored.at(l + 1, 0))

        @block.tensor
        def _(pe):
            for s in range(RING):
                pe.sem_inc(w_used[s], 1)
            transpose = nc.tensor.transpose

            def unit_half(layer, pos, more, ks, source, group, half, first, last, done=None,
                          tile_ready=lambda k: None, after_two=lambda: None):
                s = pos % RING
                if half == 0:
                    pe.wait_ge(w_hi_made[s], USES[s] * layer + pos // RING + more + 1)
                    pe.wait_ge(w_lo_made[s], USES[s] * layer + pos // RING + more + 1)
                for i, k in enumerate(ks):
                    if i == 2:
                        after_two()
                    tile_ready(k)
                    hi, lo = source(k)
                    begins, ends = first and i == 0, last and i == len(ks) - 1
                    for ct in range(2):
                        out = ps[:, 4 * group + 2 * half + ct, 0:H2]
                        wh, wl = (w[s][:, i, P * ct:P * ct + P] for w in (w_hi, w_lo))
                        pe.matmul(out, wh, hi[:, cols(half)], start=begins, stop=False)
                        pe.matmul(out, wl, hi[:, cols(half)], start=False, stop=False)
                        mm = pe.matmul(out, wh, lo[:, cols(half)], start=False, stop=ends)
                if half:
                    mm.then_inc(w_used[s], 1)
                elif done is not None:
                    mm.then_inc(done.sem, 1)

            def unit(layer, pos, more, ks, source, group, first, last, done=None, before_half=lambda half: None):
                for half in range(2):
                    before_half(half)
                    unit_half(layer, pos, more, ks, source, group, half, first, last, done)

            def from_h(k):
                return h_hi[:, k, :], h_lo[:, k, :]

            def from_mix(k):
                if k < 2:
                    return ab_hi[:, k, :], a_lo[:, k, :]
                if k < 4:
                    return ab_hi[:, k, :], b_lo[:, k - 2, :]
                return c_hi[:, k - 4, :], c_lo[:, k - 4, :]

            def from_f(k):
                return f_hi[:, k, :], f_lo[:, k, :]

            def sum_squares(layer, squares, n, sums, bank, half):
                pe.wait_ge(squares.sem, squares.at(layer, n))
                for ct in range(2):
                    mm = pe.matmul(ps[:, bank, 0:H2], ones[:], acc[:, ct, cols(half)],
                                   start=(ct == 0), stop=(ct == 1))
                mm.then_inc(sums.sem, 1)

            def normed_units(layer, norm, pos, dones, out, sum_last=lambda: None):
                for half in range(2):
                    for i in range(4):
                        def h_ready(k):
                            n = 16 * norm + 8 * half + k + 1
                            pe.wait_ge(h_hi_made.sem, h_hi_made.at(layer, n))
                            pe.wait_ge(h_lo_made.sem, h_lo_made.at(layer, n))
                        if half and i == 2:
                            pe.wait_ge(pre_root.sem, pre_root.at(layer, 2 * norm + 1))
                        kh = i % 2
                        unit_half(layer, pos + i, 0, range(4 * kh, 4 * kh + 4), from_h, i // 2, half,
                                  kh == 0, kh == 1, dones[i // 2] if kh else None, h_ready if i < 2 else (lambda k: None))
                        if half == 0 and i == 1:
                            sum_last()
                        if (half, i) == ((0, 2) if norm else (1, 0)):
                            sum_squares(layer, pre_acc, 6 * norm + 3, pre_sum, 6, 0)
                pe.wait_ge(*out)
                sum_squares(layer, pre_acc, 6 * norm + 6, pre_sum, 4, 1)

            pe.wait_ge(eps_set, 2)
            pe.wait_ge(const_landed, 16)
            for c in range(NC + 1):
                if c == NC - 1:
                    pe.wait_ge(prm_turned, 2)
                if c == NC:
                    pe.wait_ge(first_tiles_in, 1)
                    pe.wait_ge(last_tiles_in, 1)
                pe.wait_ge(x_landed[c], 16)
                m = rows_of(c)
                for k in range(KT):
                    tr = transpose(ps[:, 2 * (c % NC) + k // 4, m * (k % 4):m * (k % 4) + m],
                                   xrow[0:m, c, P * k:P * k + P], ident[0:m, 0:m])
                tr.then_inc(turned_in, 1)
                if c == 1:
                    pe.wait_ge(prm_landed, 16 * 5)
                    transpose(ps[:, 7, 0:DEPTH * NPRM], prow[:],
                              ident[0:DEPTH * NPRM, 0:DEPTH * NPRM]).then_inc(prm_turned, 1)

            with pe.Fori(0, DEPTH) as l:
                task = [0]

                def task_done(ins):
                    ins.then_inc(mix_pe.sem, 1)
                    task[0] += 1

                def after(signal, n):
                    pe.wait_ge(signal.sem, signal.at(l, n))

                def setup_weights():
                    pe.wait_ge(tables_landed.sem, tables_landed.at(l, 16 * 13))
                    pe.wait_ge(win_out.sem, win_out.at(l, 4))
                    pe.matmul(ps[:, 5, 0:512], ones[0:1, :], ln_row[:].rearrange("p a c -> p (a c)"),
                              start=True, stop=True)
                    for h in range(AHEADS):
                        tr = transpose(ps[:, 4, P * h:P * h + P], ws_in[:, h, :], ident)
                    task_done(tr)

                def setup_rows():
                    after(spatial_made, 1)
                    for hp in range(2):
                        pe.matmul(ps[:, 7, CH * hp:CH * hp + CH], cst[0:AHEADS, C_SEL + P * hp:C_SEL + P * hp + P],
                                  bs_row[:], start=True, stop=True)
                        transpose(ps[:, 7, 256 + 2 * DB * hp:256 + 2 * DB * (hp + 1)],
                                  sc_in[:, P * hp:P * hp + P], ident[0:2 * DB, 0:2 * DB])
                    first = ws_t[0:DS, :, 0:DS].rearrange("p h (o t) -> p h o t", o=1)
                    task_done(pe.matmul(ps[0:NS, 6, 0:AHEADS * NS].rearrange("p (h b t) -> p h b t", h=AHEADS, t=DS),
                                        cst[0:DS, C_REP:C_REP + NS], over(first, [DS, AHEADS, DB, DS]),
                                        start=True, stop=True))

                def turn(src, bank, dst_c, rows_bank, free):
                    free()
                    for c in range(NC):
                        transpose(ps[:, bank, P * c:P * c + P], src[:, P * c:P * c + P], ident)
                    task_done(transpose(ps[0:NS, rows_bank, dst_c:dst_c + P], src[:, SEQ:T], ident))

                def turn_k(hp):
                    def free():
                        pe.wait_ge(roped.sem, roped.at(l, hp // 2 + 1))
                        after(*((k_tok_made, hp - 1) if hp >= 2 else (setup_read, 1)))
                    turn(kT[:, hp, :], 4 + hp % 2, P * hp, 6, free)

                def turn_v(hp):
                    def free():
                        pe.wait_ge(win_out.sem, win_out.at(l, 2 * (V01 + hp // 2) + 2))
                        if hp >= 2:
                            after(v_tok_made, hp - 1)
                        else:
                            after(k_tok_made, hp + 3)
                    turn(E[(V01 + hp // 2) % 2][:, hp % 2, :], 4 + hp % 2, P * hp, 7, free)

                def turn_av():
                    pe.wait_ge(win_out.sem, win_out.at(l, 2 * AV + 2))
                    after(v_tok_made, 5)
                    after(k_tok_made, 5)
                    for c in range(NC):
                        for ct in range(2):
                            tr = transpose(ps[:, 6 + c // 2, 256 * (c % 2) + P * ct:256 * (c % 2) + P * ct + P],
                                           E[AV % 2][:, ct, P * c:P * c + P], ident)
                    task_done(tr)

                def turn_av_s():
                    after(probs_made, 1)
                    for ct in range(2):
                        tr = transpose(ps[0:NS, 4, P * ct:P * ct + P], E[AV % 2][:, ct, SEQ:T], ident)
                    task_done(tr)

                def scores(c):
                    for h in range(HEADS):
                        rows = slice(HD * (h % 2), HD * (h % 2) + HD)
                        mm = pe.matmul(ps[:, 4 + h % 2, P * (h // 2):P * (h // 2) + P],
                                       kT[rows, h // 2, P * c:P * c + P], qo[rows, h // 2, P * c:P * c + P],
                                       start=True, stop=True)
                    return mm

                def attend(c):
                    after(probs_made, c + 1)
                    if c == 0:
                        after(v_tok_made, 5)
                        after(vn_read, 1)
                    else:
                        after(q_decayed, c)
                        after(state_made, c)
                        after(o_made, c)
                        after(o_rooted, c)
                    for h in range(HEADS):
                        rows = slice(HD * (h % 2), HD * (h % 2) + HD)
                        out = ps[rows, 6, P * (h // 2):P * (h // 2) + P]
                        pe.matmul(out, v_tok[:, c, HD * h:HD * h + HD], probs[:, c % 2, by_parity(h), :],
                                  start=True, stop=(c == 0))
                        if c:
                            pe.matmul(out, st_p[rows, h // 2, :], qd[rows, h // 2, :], start=False, stop=True)
                    for h in range(HEADS):
                        rows = slice(HD * (h % 2), HD * (h % 2) + HD)
                        mm = pe.matmul(ps[rows, 7, HD * (h // 2):HD * (h // 2) + HD],
                                       k_tok[:, c, HD * h:HD * h + HD], v_tok[:, c, HD * h:HD * h + HD],
                                       start=True, stop=True)
                    return mm

                def norm_o(c):
                    n = HP * CH if c < NC else HP * NS
                    after(o_squared, c + 1)
                    after(state_made, min(c + 1, NC))
                    if c == NC:
                        after(o_rooted, NC)
                    task_done(pe.matmul(ps[:, 7, 0:n], cst[:, C_BLK:C_BLK + P],
                                        rn[:, c % 2].rearrange("p q i -> p (q i)")[:, 0:n], start=True, stop=True))

                def scores_s():
                    for h in range(HEADS):
                        rows = slice(HD * (h % 2), HD * (h % 2) + HD)
                        mm = pe.matmul(ps[0:NS, 4 + h % 2, NS * (h // 2):NS * (h // 2) + NS], kT[rows, h // 2, SEQ:T],
                                       qo[rows, h // 2, SEQ:T], start=True, stop=True)
                    return mm

                def attend_s():
                    after(probs_made, 5)
                    after(o_made, 4)
                    for hp in range(HP):
                        out = ps[0:HD, 6, 2 * NS * hp:2 * NS * hp + 2 * NS]
                        for e in range(2):
                            h = 2 * hp + e
                            pe.matmul(out[:, NS * e:NS * e + NS], v_tok[0:NS, NC, HD * h:HD * h + HD],
                                      probs_s[:, by_parity(h), :], start=(h == 0), stop=False,
                                      skip_group_check=True)
                        across = out.rearrange("p (e b t) -> p e b t", e=2, b=DB)
                        for b in range(DB):
                            pe.matmul(across[:, :, b, :], st_s[:, hp, b, :], qds[:, hp, :, b, :],
                                      start=False, stop=(b == DB - 1), skip_group_check=True)
                    after(z_last_made, 1)
                    after(probs_made, 5)
                    for ct in range(2):
                        tr = transpose(ps[0:2 + 2 * DB, 5, P * ct:P * ct + P], z_last[:, ct, :], ident)
                    task_done(tr)

                def state_s(r, banks):
                    after(values_spread, r + 1)
                    if r == 0:
                        after(z_rows_made, 1)
                    for i, hp in enumerate((2 * r, 2 * r + 1)):
                        for e in range(2):
                            h = 2 * hp + e
                            mm = pe.matmul(ps[HD * e:HD * e + HD, banks[i], 0:512],
                                           k_tok[0:NS, NC, HD * h:HD * h + HD],
                                           vexp[:, 2 * i + e].rearrange("p b e -> p (b e)"),
                                           start=True, stop=True)
                    task_done(mm)

                def mix_tokens():
                    after(probs_made, 2)
                    after(vn_made, 2)
                    for h in range(AHEADS):
                        for c in range(NC):
                            mm = pe.matmul(ps[HD * (h % 2):HD * (h % 2) + HD, 4 + h // 2, P * c:P * c + P],
                                           vn[:, c, HD * h:HD * h + HD], ws_t[:, h, :], start=True, stop=True)
                    task_done(mm)

                def mix_tokens_s():
                    after(probs_made, 3)
                    alone(pe)
                    for h in range(AHEADS):
                        mm = pe.matmul(ps[HD * (h % 2):HD * (h % 2) + HD, 4, NS * (h // 2):NS * (h // 2) + NS],
                                       vn[0:NS, NC, HD * h:HD * h + HD], ws_s[:, h, :], start=True, stop=True)
                    task_done(mm)

                def first_scores():
                    pe.wait_ge(roped.sem, roped.at(l, 4))
                    after(v_tok_made, 4)
                    task_done(scores(0))

                def chunk_step(c):
                    def run():
                        attend(c)
                        if c == 0:
                            after(vn_read, 2)
                        elif c == 1:
                            after(mixed_read, 1)
                        elif c == 2:
                            after(mixed_read, 2)
                        if c < NC - 1:
                            task_done(scores(c + 1))
                        else:
                            after(probs_made, 4)
                            alone(pe)
                            task_done(scores_s())
                    return run

                tasks = {"setup_weights": setup_weights, "setup_rows": setup_rows, "scores0": first_scores,
                         "turn_av": turn_av, "turn_av_s": turn_av_s, "mix_tokens": mix_tokens,
                         "mix_tokens_s": mix_tokens_s, "attend_s": attend_s,
                         "state_s0": lambda: state_s(0, (4, 5)), "state_s1": lambda: state_s(1, (6, 7))}
                for n in range(4):
                    tasks[f"turn_k{n}"] = lambda n=n: turn_k(n)
                    tasks[f"turn_v{n}"] = lambda n=n: turn_v(n)
                    tasks[f"chunk{n}"] = chunk_step(n)
                for n in range(NC + 1):
                    tasks[f"norm_o{n}"] = lambda n=n: norm_o(n)

                for u in range(N_WIN):
                    pair, kh = u // 2, u % 2

                    def before(half, u=u, pair=pair, kh=kh):
                        if kh == 0:
                            pe.wait_ge(win_out.sem, win_out.at(l, 2 * (pair - 1) + half + 1) if pair > 2
                                       else win_out.at(l, 2 * half + 1))
                    if u == 0:
                        normed_units(l, 0, 0, (win_done, win_done), (win_out.sem, win_out.at(l, 2)))
                    elif u >= 4:
                        unit(l, u, 0, range(4 * kh, 4 * kh + 4), from_h, 0, kh == 0, kh == 1,
                             win_done if kh else None, before)
                    for name in TASKS_AFTER.get(u, []):
                        tasks[name]()
                        assert task[0] == TASK[name]

                for n, (pair, kh) in enumerate(OUT_ORDER):
                    def before(half, pair=pair, kh=kh):
                        if kh == 0:
                            pe.wait_ge(y_made.sem, y_made.at(l, 2 * (2 * pair + half) + 2))
                    if n == 0:
                        pe.wait_ge(win_out.sem, win_out.at(l, N_WIN))
                        after(ab_hi_made, 2)
                        after(ab_lo_made, 2)
                    if n == 1:
                        after(sample_state, 4)
                        after(o_rooted, 5)
                    if n == 2:
                        after(c_hi_made, 2)
                        after(c_lo_made, 2)
                    if pair < 3:
                        unit(l, OUT0 + n, 0, range(4 * kh, 4 * kh + 4), from_mix, pair % 2,
                             kh == 0, kh == 1, wide_done if kh else None, before)

                def post_sums(norm, half):
                    sum_squares(l, post_acc, 6 * norm + 5 + half, post_sum, 2 + half, half)

                for half in range(2):
                    pe.wait_ge(y_made.sem, y_made.at(l, 2 * (6 + half) + 2))
                    for n in (6, 7):
                        kh = n - 6
                        unit_half(l, OUT0 + n, 0, range(4 * kh, 4 * kh + 4), from_mix, 1, half, kh == 0, kh == 1,
                                  wide_done if kh else None,
                                  after_two=(lambda: post_sums(0, 0)) if half and kh == 0 else (lambda: None))

                def ffn_pair(j):
                    for i, (done, out) in enumerate(((gate_done, gate_out), (up_done, up_out))):
                        for kh in range(2):
                            def before(half, kh=kh, out=out):
                                if kh == 0:
                                    pe.wait_ge(out.sem, out.at(l, j * 2 + half + 1))
                            unit(l, FFN0 + 2 * i + kh, j, range(4 * kh, 4 * kh + 4), from_h, i,
                                 kh == 0, kh == 1, done if kh else None, before)
                normed_units(l, 1, FFN0, (gate_done, up_done), (up_out.sem, up_out.at(l, 3)),
                             lambda: post_sums(0, 1))
                alone(pe)
                with pe.Fori(1, FT // 2) as j:
                    ffn_pair(j)

                def down_half(n, half, after_two=lambda: None):
                    pair, k0, nk = DOWN[n]
                    g = pair % 2
                    if k0 == 0:
                        pe.wait_ge(y_made.sem, y_made.at(l, 16 + 2 * (2 * pair + half) + 2))
                    if pair == 0 and half == 0:
                        pe.wait_ge(f_lo_made.sem, f_lo_made.at(l, min(22, k0 + 4)))
                    if pair < 2 and k0 == 0 and half == 0:
                        out = up_out if g else gate_out
                        pe.wait_ge(out.sem, out.at(l, 24))
                    ends = k0 + nk == FT
                    unit_half(l, DOWN0 + n, 0, range(k0, k0 + nk), from_f, g, half, k0 == 0, ends,
                              wide_done if ends else None, after_two=after_two)
                for n in range(N_DOWN - DOWN_TAIL):
                    for half in range(2):
                        down_half(n, half)
                for half in range(2):
                    for n in range(N_DOWN - DOWN_TAIL, N_DOWN):
                        down_half(n, half, (lambda: post_sums(1, 0)) if half and n == N_DOWN - DOWN_TAIL
                                  else (lambda: None))
                post_sums(1, 1)

            for n, (c, kq) in enumerate(OUTPUTS):
                if n == 0:
                    pe.wait_ge(x_updated.sem, x_updated.at(DEPTH, 0))
                if n in (4, 7):
                    pe.wait_ge(x_updated.sem, x_updated.at(DEPTH, 2 if n == 4 else 4))
                if n >= 8:
                    pe.wait_ge(final_out, n - 7)
                m = rows_of(c)
                for k in range(4):
                    tr = transpose(ps[0:m, output_bank(n), P * k:P * k + P], x[:, 4 * kq + k, P * c:P * c + m], ident)
                tr.then_inc(final_turned, 1)

        @block.scalar
        def _(act):
            load_chunk(act, 0)
            for i, g in enumerate((g_pre_mix, g_post_mix, g_pre_ffn, g_post_ffn)):
                act.dma_start(prow[8 * DEPTH * i:8 * DEPTH * (i + 1), :],
                              g.rearrange("l (t p) -> (l t) p", p=P)).then_inc(prm_landed, 16)
            act.dma_start(prow[DEPTH * CONV:, :],
                          conv_w.rearrange("l w (t p) -> (l w t) p", p=P)).then_inc(prm_landed, 16)
            load_chunk(act, 2)
            act.sem_inc(y_made.sem, 8)

            def split(layer, pos, more=0, nk=4):
                s = pos % RING
                act.wait_ge(w_landed[s], (USES[s] * layer + pos // RING + more + 1) * 16)
                act.activation(w_hi[s][:, 0:nk, :], w_raw[s][:, 0:nk, :], ACT.Copy).then_inc(w_hi_made[s], 1)

            for c in range(FIRST_CHUNKS):
                act.wait_ge(turned_in, c + 1)
                turned_x(c, 0, lambda dst, src: act.activation(dst, src, ACT.Copy)).then_inc(first_tiles_in, 1)
            act.wait_ge(first_tiles_in, FIRST_CHUNKS)

            with act.Fori(0, DEPTH) as l:

                def after(signal, n):
                    act.wait_ge(signal.sem, signal.at(l, n))

                def pre_half(norm, gain, half, updated, splits, pairs=range(4)):
                    for pair in pairs:
                        updated(pair)
                        for ct in range(2):
                            k = 2 * pair + ct
                            act.activation(h_hi[:, k, cols(half)], x[:, k, cols(half)], ACT.Copy,
                                           scale=prm[:, gain + k:gain + k + 1]).then_inc(h_hi_made.sem, 1)
                        for pos in splits.get(pair, []) if half == 0 else []:
                            split(l, pos)
                        if half and pair >= 2:
                            act.wait_ge(pre_acc.sem, pre_acc.at(l, 6 * norm + pair - 1))
                        act.activation(square_room(half, pair), x[:, 2 * pair:2 * pair + 2, cols(half)],
                                       ACT.Square).then_inc(pre_sq.sem, 1)

                def root_table():
                    act.activation(spare[:], eps[:], ACT.Sqrt)

                def pre_root_half(norm, half):
                    act.wait_ge(pre_sum.sem, pre_sum.at(l, 2 * norm + half + 1))
                    act.activation(r_pre[:, 0, cols(half)], ps[:, 6 - 2 * half, 0:H2], ACT.Sqrt,
                                   bias=eps[:, 0:1], scale=1.0 / D).then_inc(pre_root.sem, 1)

                def post_half(norm, pair, gain, pos, half):
                    group = pair % 2
                    pair_done(act, l, half, wide_done, 4 * norm + pair + 1, pos)
                    if pair == 0 and norm and half == 0:
                        after(f_lo_made, 22)
                    if pair >= 2:
                        act.wait_ge(post_acc.sem, post_acc.at(l, 6 * norm + 2 * (pair - 2) + half + 1))
                    squares = acc if pair == 0 else E[0]
                    act.activation(squares[:, :, cols(half)], bank_pair(group, half), ACT.Square)\
                       .then_inc(post_sq.sem, 1)
                    for ct in range(2):
                        k = 2 * pair + ct
                        act.activation(y[:, k, cols(half)], ps[:, 4 * group + 2 * half + ct, 0:H2], ACT.Copy,
                                       scale=prm[:, gain + k:gain + k + 1]).then_inc(y_made.sem, 1)

                def post_root_half(norm, half):
                    act.wait_ge(post_sum.sem, post_sum.at(l, 2 * norm + half + 1))
                    act.activation(r_post[:, 0, cols(half)], ps[:, 2 + half, 0:H2], ACT.Sqrt,
                                   bias=eps[:, 0:1], scale=1.0 / D).then_inc(post_root.sem, 1)

                split(l, 0)
                act.wait_ge(prm_ready.sem, prm_ready.at(l, 1))
                act.wait_ge(eps_set, 2)
                for half in range(2):
                    if half == 0:
                        act.wait_ge(x_ready, l + 1)
                    pre_half(0, G_PRE_MIX, half,
                             (lambda pair: act.wait_ge(x_updated.sem, x_updated.at(l, pair + 1))) if half
                             else (lambda pair: None), {1: [1], 2: [2], 3: [3]})

                def swap(pair, n):
                    act.wait_ge(win_out.sem, win_out.at(l, 2 * pair + (3 if pair == 0 else 2)))
                    if n:
                        act.wait_ge(roped.sem, roped.at(l, n))
                    for qd_ in range(4):
                        to = 32 * (qd_ ^ 1)
                        ins = act.activation(acc[to:to + 32], E[pair % 2][32 * qd_:32 * qd_ + 32], ACT.Copy)
                    ins.then_inc(swapped.sem, 1)

                def v_tok_out(hp):
                    after(mix_pe, TASK[f"turn_v{hp}"])
                    act.activation(v_tok[:, 0:NC, P * hp:P * hp + P],
                                   ps[:, 4 + hp % 2, :].rearrange("p (c f) -> p c f", c=NC), ACT.Copy)\
                       .then_inc(v_tok_made.sem, 1)
                    if hp == HP - 1:
                        act.activation(v_tok[0:NS, NC, :], ps[0:NS, 7, :], ACT.Copy).then_inc(v_tok_made.sem, 1)

                def o_out(c):
                    after(mix_pe, TASK[f"chunk{c}" if c < NC else "attend_s"])
                    if c == NC:
                        o = ps[0:HD, 6, 0:HEADS * NS].rearrange("p (q e i) -> p q e i", q=HP, e=2)
                        after(o_normed, c - 1)
                        for e in range(2):
                            squares = rn[HD * e:HD * e + HD, 0].rearrange("p q i -> p (q i)")[:, 0:HP * NS]
                            ins = act.activation(squares.rearrange("p (q i) -> p q i", q=HP), o[:, :, e], ACT.Square)
                        ins.then_inc(o_squared.sem, 1)
                        after(q_decayed, c)
                        for e in range(2):
                            ins = act.activation(qo[HD * e:HD * e + HD, :, SEQ:T], o[:, :, e], ACT.Copy)
                        ins.then_inc(o_made.sem, 1)
                        return
                    m = CH
                    o = ps[:, 6, 0:HP * m].rearrange("p (q i) -> p q i", q=HP)
                    if c >= 2:
                        after(o_normed, c - 1)
                    squares = rn[:, c % 2].rearrange("p q i -> p (q i)")[:, 0:HP * m]
                    act.activation(squares, ps[:, 6, 0:HP * m], ACT.Square).then_inc(o_squared.sem, 1)
                    if c:
                        after(q_decayed, c)
                    act.activation(qo[:, :, CH * c:CH * c + m], o, ACT.Copy).then_inc(o_made.sem, 1)

                def o_root(c):
                    after(mix_pe, TASK[f"norm_o{c}"])
                    n = HP * (CH if c < NC else NS)
                    act.activation(rn[:, c % 2].rearrange("p q i -> p (q i)")[:, 0:n], ps[:, 7, 0:n], ACT.Sqrt,
                                   bias=eps[:, 0:1]).then_inc(o_rooted.sem, 1)

                def ln_root(m, chunks, n):
                    after(ln_stats, n)
                    act.activation(rstd[0:m, chunks], mv[0:m, chunks, 1], ACT.Sqrt, bias=eps[0:m, 0:1])\
                       .then_inc(ln_rooted.sem, 1)

                for u in range(2, N_WIN):
                    if u == 2:
                        pre_root_half(0, 0)
                    split(l, u + LEAD)
                    pair, kh = u // 2, u % 2
                    if u == 3:
                        pre_root_half(0, 1)
                    if u in (4, 5):
                        swap(u - 4, u - 4)
                    if kh and pair in (Q01, Q23):
                        swap(pair, pair - Q01 + 2)
                    for hp in range(HP):
                        if f"turn_v{hp}" in TASKS_AFTER.get(u, []):
                            v_tok_out(hp)
                    if u == 14:
                        ln_root(P, slice(0, NC), 1)
                    if u == 15:
                        ln_root(NS, slice(NC, NC + 1), 2)
                    if u in (16, 18, 20, 22):
                        o_out((u - 16) // 2)
                    if u in (17, 19, 21, 23):
                        o_root((u - 17) // 2)
                    if u == 20:
                        after(a_made, 2)
                        act.activation(ab_hi[:, 0:2, :], a_u[:], ACT.Copy).then_inc(ab_hi_made.sem, 1)
                    if u == 21:
                        after(z_made, 1)
                        act.activation(z_last[:, :, 0:2], z_p[:, :, SEQ:SEQ + 2], ACT.Copy)
                        for ct in range(2):
                            ins = act.activation(z_last[:, ct, 2:].rearrange("p (b w) -> p b w", w=2),
                                                 z_s[:, ct, :, DS:DS + 2], ACT.Copy)
                        ins.then_inc(z_last_made.sem, 1)
                    if u == 23:
                        o_out(NC)
                        after(b_made, 1)
                        act.activation(ab_hi[:, 2:4, :], b_b[:], ACT.Copy).then_inc(ab_hi_made.sem, 1)
                    if u == 24:
                        o_root(NC)
                for pair in (G01, G23):
                    act.wait_ge(win_out.sem, win_out.at(l, 2 * pair + 2))
                    act.activation(sg[:, 2 * (pair - G01):2 * (pair - G01) + 2, :], E[pair % 2][:], ACT.Silu)\
                       .then_inc(silu_g.sem, 1)
                root_table()
                for i in range(2):
                    after(c_made, i + 1)
                    act.activation(c_hi[:, 2 * i:2 * i + 2, :], qo[:, 2 * i:2 * i + 2, :], ACT.Copy)\
                       .then_inc(c_hi_made.sem, 1)

                def pre_ffn(half, pairs):
                    pre_half(1, G_PRE_FFN, half,
                             lambda pair: act.wait_ge(x_updated.sem, x_updated.at(l, 4 + 4 * half + pair + 1)),
                             {2: [FFN0 + 2], 3: [FFN0 + 3]}, pairs)
                for n in range(N_WOUT):
                    split(l, OUT0 + n + LEAD)
                    if n in OUT_LAST:
                        for half in range(2):
                            post_half(0, OUT_LAST[n], G_POST_MIX, OUT0 + n, half)
                            if n == N_WOUT - 1 and half == 0:
                                post_root_half(0, 0)
                                pre_ffn(0, [0])
                pre_ffn(0, range(1, 4))
                post_root_half(0, 1)
                pre_ffn(1, range(4))

                def ffn_pair(j, first):
                    if first:
                        pre_root_half(1, 0)
                    else:
                        split(l, FFN0 + 2, j)
                        split(l, FFN0 + 3, j)
                    if first:
                        split(l, FFN0 + 4, j)
                        split(l, FFN0 + 5, j)
                        pre_root_half(1, 1)
                    for half in range(2):
                        act.wait_ge(gate_out.sem, gate_out.at(l, j * 2 + half + 1 + 2))
                        act.activation(E[1][:, :, cols(half)], E[0][:, :, cols(half)], ACT.Silu)\
                           .then_inc(silu_made.sem, 1)
                    if not first:
                        split(l, FFN0 + 4, j)
                        split(l, FFN0 + 5, j)
                    for half in range(2):
                        act.wait_ge(f_made.sem, f_made.at(l, j * 2 + half + 1))
                        act.activation(f_hi[:, bass.ds(j * 2, 2), cols(half)], acc[:, :, cols(half)], ACT.Copy)\
                           .then_inc(f_hi_made.sem, 1)
                after(stored, stored.per)
                ffn_pair(0, True)
                with act.Fori(1, FT // 2) as j:
                    ffn_pair(j, False)

                root_table()
                for n, (pair, k0, nk) in enumerate(DOWN):
                    if n + LEAD < N_DOWN:
                        split(l, DOWN0 + n + LEAD, nk=DOWN[n + LEAD][2])
                    if k0 + nk == FT:
                        for half in range(2):
                            post_half(1, pair, G_POST_FFN, DOWN0 + n, half)
                            if pair == 3:
                                post_root_half(1, half)

            act.wait_ge(stored.sem, stored.at(DEPTH, 0))
            for n in BY_SCALAR:
                rows_out(act, n, lambda dst, src: act.activation(dst, src, ACT.Copy), final_out)

        @block.vector
        def _(vec):
            vec.sem_inc(gate_out.sem, 2)
            vec.sem_inc(up_out.sem, 2)

            def split(layer, pos, more=0, nk=4):
                s = pos % RING
                vec.wait_ge(w_hi_made[s], USES[s] * layer + pos // RING + more + 1)
                vec.tensor_tensor(w_lo[s][:, 0:nk, :], w_raw[s][:, 0:nk, :], w_hi[s][:, 0:nk, :], ALU.subtract)\
                   .then_inc(w_lo_made[s], 1)

            for c in range(NC + 1):
                vec.wait_ge(turned_in, c + 1)
                if c >= FIRST_CHUNKS:
                    turned_x(c, 0, vec.tensor_copy)
                turned_x(c, 1, vec.tensor_copy).then_inc(last_tiles_in, 1)
                if c == 1:
                    vec.wait_ge(prm_turned, 1)
                    vec.tensor_copy(prm_all[:], ps[:, 7, 0:DEPTH * NPRM]).then_inc(prm_turned, 1)
                if c == FIRST_CHUNKS - 1:
                    vec.wait_ge(last_tiles_in, FIRST_CHUNKS)
                    vec.sem_inc(x_ready, 1)
            vec.wait_ge(last_tiles_in, NC + 1)
            vec.sem_inc(mix_free, 1)

            def recip_post(layer, n, y_tiles, half):
                vec.wait_ge(post_root.sem, post_root.at(layer, n) + 2)
                vec.reciprocal(r_post[:, 0, cols(half)], r_post[:, 0, cols(half)]).then_inc(r_post_made.sem, 1)
                vec.wait_ge(r_post_made.sem, r_post_made.at(layer, n + 1))
                vec.wait_ge(y_made.sem, y_made.at(layer, y_tiles) + 8)

            def update(layer, half, between=lambda pair: None):
                def pair_of(buf, pair):
                    return buf[:, 2 * pair:2 * pair + 2, cols(half)]

                def scale(pair):
                    yy = pair_of(y, pair)
                    return vec_own.mark(vec.tensor_tensor(yy, yy, over(r_post[:, :, cols(half)], [P, 2, H2]),
                                                          ALU.mult))
                scaled = scale(0)
                for pair in range(4):
                    vec.wait_ge(vec_own.sem, vec_own.at(layer, scaled))
                    vec.tensor_tensor(pair_of(x, pair), pair_of(x, pair), pair_of(y, pair), ALU.add)\
                       .then_inc(x_updated.sem, 1)
                    if pair < 3:
                        scaled = scale(pair + 1)
                    between(pair)

            with vec.Fori(0, DEPTH) as l:
                vec_own.n = 0

                def after(signal, n):
                    vec.wait_ge(signal.sem, signal.at(l, n))

                def then(ins):
                    after(vec_own, vec_own.mark(ins))

                def low_tiles(norm, gain, half, pair):
                    for k in (2 * pair, 2 * pair + 1):
                        vec.wait_ge(h_hi_made.sem, h_hi_made.at(l, 16 * norm + 8 * half + k + 1))
                        vec.scalar_tensor_tensor(h_lo[:, k, cols(half)], x[:, k, cols(half)],
                                                 prm[:, gain + k:gain + k + 1], h_hi[:, k, cols(half)],
                                                 ALU.mult, ALU.subtract).then_inc(h_lo_made.sem, 1)

                def add_squares(norm, half):
                    for pair in range(1, 4):
                        n = 6 * norm + 3 * half + pair
                        vec.wait_ge(pre_sq.sem, pre_sq.at(l, 8 * norm + 4 * half + pair + 1))
                        if pair > 1:
                            vec.wait_ge(pre_acc.sem, pre_acc.at(l, n - 1))
                        vec.tensor_tensor(acc[:, :, cols(half)], acc[:, :, cols(half)],
                                          square_room(half, pair), ALU.add).then_inc(pre_acc.sem, 1)

                def recip_pre(norm, half):
                    vec.wait_ge(pre_root.sem, pre_root.at(l, 2 * norm + half + 1))
                    vec.reciprocal(r_pre[:, 0, cols(half)], r_pre[:, 0, cols(half)]).then_inc(r_pre_made.sem, 1)
                    vec.wait_ge(r_pre_made.sem, r_pre_made.at(l, 2 * norm + half + 1))

                def scaled_out(dst, group, half, out, done, n, pos, more=0):
                    pair_done(vec, l, half, done, n, pos, more)
                    vec.tensor_tensor(dst[:, :, cols(half)], bank_pair(group, half),
                                      over(r_pre[:, :, cols(half)], [P, 2, H2]), ALU.mult).then_inc(out.sem, 1)

                def post_add(norm, pair, half):
                    n = 6 * norm + 2 * (pair - 1) + half
                    vec.wait_ge(post_sq.sem, post_sq.at(l, 8 * norm + 2 * pair + half + 1))
                    if pair > 1:
                        vec.wait_ge(post_acc.sem, post_acc.at(l, n - 1))
                    vec.tensor_tensor(acc[:, :, cols(half)], acc[:, :, cols(half)], E[0][:, :, cols(half)],
                                      ALU.add).then_inc(post_acc.sem, 1)

                vec.wait_ge(prm_turned, 2)
                vec.wait_ge(y_made.sem, y_made.at(l, 0) + 8)
                gains = prm_all[:, 0:DEPTH * CONV].rearrange("p (i l t) -> p i l t", i=4, l=DEPTH)
                vec.tensor_copy(prm[:, 0:CONV].rearrange("p (i o t) -> p i o t", i=4, o=1),
                                gains[:, :, bass.ds(l, 1), :])
                taps = prm_all[:, DEPTH * CONV:].rearrange("p (l n) -> p l n", l=DEPTH)
                vec.tensor_copy(prm[:, CONV:NPRM].rearrange("p (o n) -> p o n", o=1), taps[:, bass.ds(l, 1), :])\
                   .then_inc(prm_ready.sem, 1)
                split(l, 0)
                for pair in range(4):
                    low_tiles(0, G_PRE_MIX, 0, pair)
                    if pair:
                        split(l, pair)
                recip_post(l, 0, 0, 1)

                def then_low(pair):
                    if pair == 1:
                        add_squares(0, 0)
                    low_tiles(0, G_PRE_MIX, 1, pair)
                update(l, 1, then_low)
                add_squares(0, 1)

                def rope(pair, n, dst):
                    hp = 2 * (n % 2)
                    cos = over(tab[:, T_COS:T_COS + T].rearrange("p (o t) -> p o t", o=1), [P, 2, T])
                    sin = over(tab[:, T_SIN:T_SIN + T].rearrange("p (o t) -> p o t", o=1), [P, 2, T])
                    out = dst[:, hp:hp + 2, :]
                    vec.tensor_tensor(out, E[pair % 2][:], cos, ALU.mult)
                    vec.wait_ge(swapped.sem, swapped.at(l, n + 1))
                    then(vec.tensor_tensor(acc[:], acc[:], sin, ALU.mult))
                    vec.tensor_tensor(out, out, acc[:], ALU.add).then_inc(roped.sem, 1)

                def k_tok_out(hp):
                    after(mix_pe, TASK[f"turn_k{hp}"])
                    kdec = cst[:, C_KDEC + 2 * hp:C_KDEC + 2 * hp + 2]
                    for e in range(2):
                        ins = vec.tensor_scalar(
                            k_tok[:, 0:NC, P * hp + HD * e:P * hp + HD * e + HD],
                            ps[:, 4 + hp % 2, :].rearrange("p (c f) -> p c f", c=NC)[:, :, HD * e:HD * e + HD],
                            kdec[:, e:e + 1], None, ALU.mult)
                    ins.then_inc(k_tok_made.sem, 1)
                    if hp == HP - 1:
                        vec.tensor_tensor(
                            k_tok[0:NS, NC, :].rearrange("p (h d) -> p h d", h=HEADS),
                            ps[0:NS, 6, :].rearrange("p (h d) -> p h d", h=HEADS),
                            over(cst[0:NS, C_KDECS:C_KDECS + HEADS].rearrange("p (h o) -> p h o", o=1),
                                 [NS, HEADS, HD]), ALU.mult).then_inc(k_tok_made.sem, 1)

                def probs_out(c):
                    after(mix_pe, TASK[f"chunk{c - 1}" if c else "scores0"])
                    vec.tensor_tensor(probs[:, c % 2].rearrange("p h i -> p (h i)"),
                                           ps[:, 4:6, :].rearrange("p b i -> p (b i)"),
                                           tab[:, T_DM:T_DM + 1024], ALU.mult).then_inc(probs_made.sem, 1)

                def q_decay(c):
                    qdec = tab[:, T_QD:T_QD + HP * CH].rearrange("p (q i) -> p q i", q=HP)
                    vec.tensor_tensor(qd[:], qo[:, :, P * c:P * c + P], qdec, ALU.mult).then_inc(q_decayed.sem, 1)

                def state_out(c):
                    upd = ps[:, 7, 0:HP * HD].rearrange("p (q e) -> p q e", q=HP)
                    if c == 0:
                        vec.tensor_copy(st_p[:], upd).then_inc(state_made.sem, 1)
                        return
                    dec = over(cst[:, C_CDEC:C_CDEC + HP].rearrange("p (q o) -> p q o", o=1), [P, HP, HD])
                    then(vec.tensor_tensor(st_p[:], st_p[:], dec, ALU.mult))
                    vec.tensor_tensor(st_p[:], st_p[:], upd, ALU.add).then_inc(state_made.sem, 1)

                def o_norm(c):
                    m = CH if c < NC else NS
                    r = rn[:, c % 2].rearrange("p q i -> p (q i)")[:, 0:HP * m]
                    oo = qo[:, :, CH * c:CH * c + m]
                    after(o_rooted, c + 1)
                    then(vec.reciprocal(r, r))
                    vec.tensor_tensor(oo, oo, r.rearrange("p (q i) -> p q i", q=HP), ALU.mult)\
                       .then_inc(o_normed.sem, 1)

                def norm_stats(chunks, src, m, n):
                    for c in chunks:
                        ins = vec.bn_stats(bn[0:m, c, :], src(c))
                    n_own = vec_own.mark(ins)
                    after(vec_own, n_own)
                    alone(vec)
                    for c in chunks:
                        ins = vec.bn_aggr(mv[0:m, c, :], bn[0:m, c, :])
                    ins.then_inc(ln_stats.sem, 1)

                def norm_rows(chunks, src, m, n):
                    part = slice(chunks[0], chunks[-1] + 1)
                    after(ln_rooted, n)
                    then(vec.reciprocal(rstd[0:m, part], rstd[0:m, part]))
                    for c in chunks:
                        ins = vec.tensor_scalar(vn[0:m, c, :], src(c), mv[0:m, c, 0:1], rstd[0:m, c:c + 1],
                                                ALU.subtract, ALU.mult)
                    ins.then_inc(vn_read.sem, 1)
                    after(vn_read, n)
                    shape = [m, len(chunks), AW]
                    then(vec.tensor_tensor(vn[0:m, part, :], vn[0:m, part, :],
                                           over(ln[0:m, 0:1, :], shape), ALU.mult))
                    vec.tensor_tensor(vn[0:m, part, :], vn[0:m, part, :], over(ln[0:m, 1:2, :], shape), ALU.add)\
                       .then_inc(vn_made.sem, 1)

                def expand(r):
                    for i in range(4):
                        h = 4 * r + i
                        v = v_tok[0:NS, NC, HD * h:HD * h + HD].rearrange("p (o e) -> p o e", o=1)
                        m = cst[0:NS, C_BMASK:C_BMASK + DB].rearrange("p (b o) -> p b o", o=1)
                        ins = vec.tensor_tensor(vexp[:, i], over(v, [NS, DB, HD]), over(m, [NS, DB, HD]), ALU.mult)
                    ins.then_inc(values_spread.sem, 1)

                def state_s_out(r, banks):
                    for i, hp in enumerate((2 * r, 2 * r + 1)):
                        ins = vec.scalar_tensor_tensor(
                            st_s[:, hp].rearrange("p b e -> p (b e)"), st_s[:, hp].rearrange("p b e -> p (b e)"),
                            cst[:, C_CDECS + hp:C_CDECS + hp + 1], ps[:, banks[i], 0:512], ALU.mult, ALU.add)
                        ins.then_inc(sample_state.sem, 1)

                prompt_rows = (range(NC), lambda c: ps[:, 6 + c // 2, 256 * (c % 2):256 * (c % 2) + 256], P, 1)
                sample_rows = (range(NC, NC + 1), lambda c: ps[0:NS, 4, 0:AW], NS, 2)
                for u in range(2, N_WIN):
                    pair, kh = u // 2, u % 2
                    if u in (2, 3):
                        recip_pre(0, u - 2)
                        scaled_out(E[K01], 0, u - 2, win_out, win_done, 1, 1)
                        scaled_out(E[K23], 1, u - 2, win_out, win_done, 2, 3)
                    split(l, u + LEAD)
                    if u == 3:
                        vec.wait_ge(win_out.sem, win_out.at(l, 4))
                        vec.wait_ge(tables_landed.sem, tables_landed.at(l, 16 * 13))
                    elif kh:
                        if pair in (V01, V23):
                            vec.wait_ge(swapped.sem, swapped.at(l, pair - V01 + 1))
                        if pair in (Q01, Q23):
                            after(mix_pe, TASK["turn_v1" if pair == Q01 else "turn_v3"])
                        if pair == AV:
                            vec.wait_ge(swapped.sem, swapped.at(l, 3))
                        if pair == BC:
                            vec.wait_ge(swapped.sem, swapped.at(l, 4))
                        if pair == BX:
                            after(mix_pe, TASK["turn_av_s"])
                        if pair == G01:
                            after(b_made, 1)
                        dst = {AU: a_u, BB: b_b}.get(pair, E[pair % 2])
                        for half in range(2):
                            scaled_out(dst, 0, half, win_out, win_done, pair + 1, 2 * pair + 1)
                        vec.wait_ge(win_out.sem, win_out.at(l, 2 * pair + 2))
                    if u == 4:
                        rope(K01, 0, kT)
                        vec.wait_ge(z_zeroed.sem, z_zeroed.at(l, 1))
                        after(mix_pe, TASK["setup_weights"])
                        vec.tensor_tensor(ws_t[:], ps[:, 4, :].rearrange("p (h i) -> p h i", h=AHEADS),
                                          over(tab[:, T_TRIL:T_TRIL + P].rearrange("p (o i) -> p o i", o=1),
                                               [P, AHEADS, CH]), ALU.mult).then_inc(spatial_made.sem, 1)
                        vec.tensor_copy(ln[:].rearrange("p a c -> p (a c)"), ps[:, 5, :])
                    if u == 5:
                        after(mix_pe, TASK["setup_rows"])
                        vec.tensor_copy(bs[:].rearrange("p a c -> p (a c)"), ps[:, 7, 0:256])
                        for ct in range(2):
                            vec.tensor_copy(z_s[:, ct, :, 0:2],
                                            ps[:, 7, 256 + 2 * DB * ct:256 + 2 * DB * (ct + 1)]
                                            .rearrange("p (b w) -> p b w", w=2))
                        vec.tensor_tensor(ws_s[:], ps[0:NS, 6, 0:NS * AHEADS].rearrange("p (h i) -> p h i", h=AHEADS),
                                          over(tab[0:NS, T_TRILS:T_TRILS + NS].rearrange("p (o i) -> p o i", o=1),
                                               [NS, AHEADS, NS]), ALU.mult).then_inc(setup_read.sem, 1)
                        after(setup_read, 1)
                        rope(K23, 1, kT)
                    if kh and pair in (Q01, Q23):
                        rope(pair, pair - Q01 + 2, qo)
                    for hp in range(HP):
                        if f"turn_k{hp}" in TASKS_AFTER.get(u, []):
                            k_tok_out(hp)
                    if u == 13:
                        probs_out(0)
                    if u == 14:
                        after(mix_pe, TASK["turn_av"])
                        norm_stats(*prompt_rows)
                    if u == 15:
                        norm_rows(*prompt_rows)
                        after(mix_pe, TASK["turn_av_s"])
                        norm_stats(*sample_rows)
                        norm_rows(*sample_rows)
                    if u in (16, 18, 20):
                        c = (u - 16) // 2
                        probs_out(c + 1)
                        q_decay(c + 1)
                        state_out(c)
                    if u in (17, 19, 21, 23):
                        o_norm((u - 17) // 2)
                    if u == 17:
                        after(mix_pe, TASK["mix_tokens"])
                        mixed = ps[:, 4:6, :].rearrange("p h (c i) -> p h c i", c=NC)
                        for hp in range(2):
                            ins = vec.tensor_tensor(E[1][:, hp, 0:SEQ].rearrange("p (c i) -> p c i", c=NC),
                                                    mixed[:, hp], over(bs[:, hp:hp + 1, :], [P, NC, CH]), ALU.add)
                        ins.then_inc(mixed_read.sem, 1)
                        after(mixed_read, 1)
                        vec.tensor_tensor(a_u[:, :, 0:SEQ], a_u[:, :, 0:SEQ], E[1][:, :, 0:SEQ], ALU.mult)\
                           .then_inc(a_made.sem, 1)
                    if u == 19:
                        after(mix_pe, TASK["mix_tokens_s"])
                        for hp in range(2):
                            ins = vec.tensor_tensor(E[0][:, hp, 0:NS].rearrange("p (b t) -> p b t", t=DS),
                                                    ps[:, 4, NS * hp:NS * hp + NS].rearrange("p (b t) -> p b t", t=DS),
                                                    over(bs[:, hp:hp + 1, 0:DS], [P, DB, DS]), ALU.add)
                        ins.then_inc(mixed_read.sem, 1)
                        after(mixed_read, 2)
                        vec.tensor_tensor(a_u[:, :, SEQ:T], a_u[:, :, SEQ:T], E[0][:, :, 0:NS], ALU.mult)\
                           .then_inc(a_made.sem, 1)
                    if u == 21:
                        zi = [E[BC % 2], E[BX % 2]]
                        vec.tensor_tensor(z_p[:, :, 2:], zi[0][:, :, 0:SEQ], zi[1][:, :, 0:SEQ], ALU.mult)
                        for ct in range(2):
                            ins = vec.tensor_tensor(z_s[:, ct, :, 2:],
                                                    zi[0][:, ct, SEQ:T].rearrange("p (b t) -> p b t", t=DS),
                                                    zi[1][:, ct, SEQ:T].rearrange("p (b t) -> p b t", t=DS), ALU.mult)
                        ins.then_inc(z_made.sem, 1)
                        for hp in range(HP):
                            qdec = tab[:, T_QDS + 2 * DS * hp:T_QDS + 2 * DS * (hp + 1)]
                            q = qo[:, hp, SEQ:T].rearrange("p (o b t) -> p o b t", o=1, t=DS)
                            ins = vec.tensor_tensor(qds[:, hp], over(q, [P, 2, DB, DS]),
                                                    over(qdec.rearrange("p (e o t) -> p e o t", e=2, o=1), [P, 2, DB, DS]),
                                                    ALU.mult)
                        ins.then_inc(q_decayed.sem, 1)
                    if u == 22:
                        after(mix_pe, TASK["chunk3"])
                        state_out(3)
                        vec.tensor_tensor(probs_s[:].rearrange("p (e q) i -> p e (q i)", e=2), ps[0:NS, 4:6, 0:HP * NS],
                                          tab[0:NS, T_DMS:T_DMS + 256].rearrange("p (e r) -> p e r", e=2), ALU.mult)\
                                             .then_inc(probs_made.sem, 1)
                        expand(0)
                        after(z_made, 1)
                        out = E[BC % 2]
                        for tap in range(3):
                            for ct in range(2):
                                w = prm[:, CONV + 2 * tap + ct:CONV + 2 * tap + ct + 1]
                                pairs = ((out[:, ct, 0:SEQ], z_p[:, ct, tap:tap + SEQ]),
                                         (out[:, ct, SEQ:T].rearrange("p (b t) -> p b t", t=DS),
                                          z_s[:, ct, :, tap:tap + DS]))
                                for o, z in pairs:
                                    if tap == 0:
                                        ins = vec.tensor_scalar(o, z, w, None, ALU.mult)
                                    else:
                                        ins = vec.scalar_tensor_tensor(o, z, w, o, ALU.mult, ALU.add)
                            then(ins)
                        vec.tensor_tensor(b_b[:], b_b[:], out[:], ALU.mult).then_inc(b_made.sem, 1)
                        after(ab_hi_made, 1)
                        vec.tensor_tensor(a_lo[:], a_u[:], ab_hi[:, 0:2, :], ALU.subtract)\
                           .then_inc(ab_lo_made.sem, 1)

                    if u == 23:
                        after(mix_pe, TASK["attend_s"])
                        vec.tensor_copy(z_rows[:], ps[0:2 + 2 * DB, 5, 0:BW]).then_inc(z_rows_made.sem, 1)
                        after(ab_hi_made, 2)
                        vec.tensor_tensor(b_lo[:], b_b[:], ab_hi[:, 2:4, :], ALU.subtract)\
                           .then_inc(ab_lo_made.sem, 1)
                    if u == 24:
                        o_norm(NC)
                        after(mix_pe, TASK["state_s0"])
                        expand(1)
                        state_s_out(0, (4, 5))
                    if u == 25:
                        after(mix_pe, TASK["state_s1"])
                        state_s_out(1, (6, 7))
                for i in range(2):
                    after(silu_g, i + 1)
                    oo = qo[:, 2 * i:2 * i + 2, :]
                    vec.tensor_tensor(oo, oo, sg[:, 2 * i:2 * i + 2, :], ALU.mult).then_inc(c_made.sem, 1)
                for i in range(2):
                    after(c_hi_made, i + 1)
                    vec.tensor_tensor(c_lo[:, 2 * i:2 * i + 2, :], qo[:, 2 * i:2 * i + 2, :],
                                      c_hi[:, 2 * i:2 * i + 2, :], ALU.subtract).then_inc(c_lo_made.sem, 1)

                for n in range(N_WOUT):
                    split(l, OUT0 + n + LEAD)
                    if OUT_LAST.get(n, 0) in (1, 2):
                        for half in range(2):
                            post_add(0, OUT_LAST[n], half)
                for half in range(2):
                    if half == 0:
                        post_add(0, 3, 0)
                    recip_post(l, 1 + half, 14 + 2 * half, half)

                    def then_low(pair):
                        if half == 0 and pair == 3:
                            split(l, FFN0 + 2)
                        low_tiles(1, G_PRE_FFN, half, pair)
                    update(l, half, then_low)
                    if half == 0:
                        post_add(0, 3, 1)
                        split(l, FFN0 + 3)
                    add_squares(1, half)

                def ffn_pair(j, first):
                    if first:
                        recip_pre(1, 0)
                        scaled_out(E[0], 0, 0, gate_out, gate_done, j + 1, FFN0 + 1, j)
                        scaled_out(acc, 1, 0, up_out, up_done, j + 1, FFN0 + 3, j)
                        split(l, FFN0 + 4, j)
                        split(l, FFN0 + 5, j)
                        recip_pre(1, 1)
                        scaled_out(E[0], 0, 1, gate_out, gate_done, j + 1, FFN0 + 1, j)
                    else:
                        split(l, FFN0 + 2, j)
                        split(l, FFN0 + 3, j)
                        for half in range(2):
                            scaled_out(E[0], 0, half, gate_out, gate_done, j + 1, FFN0 + 1, j)
                        split(l, FFN0 + 4, j)
                        split(l, FFN0 + 5, j)
                    for half in range(2):
                        if not first or half:
                            scaled_out(acc, 1, half, up_out, up_done, j + 1, FFN0 + 3, j)
                        vec.wait_ge(silu_made.sem, silu_made.at(l, j * 2 + half + 1))
                        vec.wait_ge(up_out.sem, up_out.at(l, j * 2 + half + 1 + 2))
                        vec.tensor_tensor(acc[:, :, cols(half)], acc[:, :, cols(half)], E[1][:, :, cols(half)],
                                          ALU.mult).then_inc(f_made.sem, 1)
                    for half in range(2):
                        vec.wait_ge(f_hi_made.sem, f_hi_made.at(l, j * 2 + half + 1))
                        vec.tensor_tensor(f_lo[:, bass.ds(j * 2, 2), cols(half)], acc[:, :, cols(half)],
                                          f_hi[:, bass.ds(j * 2, 2), cols(half)], ALU.subtract)\
                           .then_inc(f_lo_made.sem, 1)
                after(stored, stored.per)
                ffn_pair(0, True)
                with vec.Fori(1, FT // 2) as j:
                    ffn_pair(j, False)

                for n, (pair, k0, nk) in enumerate(DOWN):
                    if n + LEAD < N_DOWN:
                        split(l, DOWN0 + n + LEAD, nk=DOWN[n + LEAD][2])
                    if k0 + nk == FT:
                        for half in range(2) if pair in (1, 2) else ():
                            post_add(1, pair, half)
                post_add(1, 3, 0)
                recip_post(l, 3, 30, 0)
                update(l, 0, lambda pair: post_add(1, 3, 1) if pair == 1 else None)
                vec.wait_ge(x_updated.sem, x_updated.at(l, 16))
                vec.sem_inc(x_ready, 1)
                vec.sem_inc(mix_free, 1)
                assert vec_own.n == vec_own.per, vec_own.n

            vec_own.n = 0
            recip_post(DEPTH, 0, 0, 1)
            update(DEPTH, 1)
            vec.wait_ge(stored.sem, stored.at(DEPTH, 0))
            for n in BY_VECTOR:
                rows_out(vec, n, vec.tensor_copy, final_out_vec)


_INS = ["x_prompt", "x_sample", "state_ret", "state_conv", "w_in", "w_out", "w_s", "b_s", "ln_g", "ln_b", "conv_w",
        "g_pre_mix", "g_post_mix", "g_pre_ffn", "g_post_ffn", "w_gate", "w_up", "w_down"]
_OUTS = [(1, SEQ, D), (DB, DS, D), (DEPTH, 1, HEADS, HD, HD), (DEPTH, DB, HEADS, HD, HD),
         (DEPTH, 1, 2, BW), (DEPTH, DB, 2, BW), (DEPTH, DB, DS, AHEADS, HD)]


def kernel(**inputs):
    import concourse.bacc as bacc
    from concourse.bass_utils import run_bass_kernel_spmd

    nc = bacc.Bacc("TRN2", target_bir_lowering=False, num_devices=1)
    named = {n: np.ascontiguousarray(inputs[n]) for n in _INS}
    named["const"], named["table"] = tables()
    arrays, args = {}, []
    for name, a in named.items():
        arrays[f"in_{name}"] = a
        args.append(nc.dram_tensor(f"in_{name}", a.shape, mybir.dt.from_np(a.dtype), kind="ExternalInput").ap())
    for i, shape in enumerate(_OUTS):
        args.append(nc.dram_tensor(f"out_{i}", shape, F32, kind="ExternalOutput").ap())
    build(nc, *args)
    r = run_bass_kernel_spmd(nc, [arrays], core_ids=[0])
    return tuple(r.results[0][f"out_{i}"] for i in range(len(_OUTS)))
```
